# Optimizing a Trainium2 kernel written in Bass

```python
import math
import jax, jax.numpy as jnp
from jax import lax
import numpy as np

D_MODEL = 2048
BATCH = 1
SEQ = 256
DEPTH = 1

S5_WIDTH = D_MODEL // 2
S5_GROUP = 16
S5_GROUPS = S5_WIDTH // S5_GROUP
S5_STATE = 64
DT_MIN = 1e-3
DT_MAX = 1e-1
RET_HEADS = 4
RET_QK_DIM = D_MODEL // 8
RET_V_DIM = 2 * RET_QK_DIM
RET_QK_WIDTH = RET_HEADS * RET_QK_DIM
RET_V_WIDTH = RET_HEADS * RET_V_DIM
RET_CHUNK = 128
ROPE_BASE = 10000.0
MEM_LEN = 256
XATTN_HEADS = 4
XATTN_HEAD_DIM = D_MODEL // XATTN_HEADS
D_FF = 256 * ((8 * D_MODEL // 3 + 255) // 256)
N_IN = S5_WIDTH + 2 * RET_QK_WIDTH + 2 * RET_V_WIDTH + 2 * D_MODEL
RMS_EPS = 1e-6
GN_EPS = 1e-5

kernel_name = "hybrid_s5_retention_gated_macaron"

def rms_norm(x, g):
    xf = x.astype(jnp.float32)
    y = xf * lax.rsqrt(jnp.mean(xf * xf, axis=-1, keepdims=True) + RMS_EPS)
    return (y * g.astype(jnp.float32)).astype(x.dtype)

def swiglu(h, w1, w3, w2):
    return (jax.nn.silu(h @ w1) * (h @ w3)) @ w2

def _complex_affine_combine(e1, e2):
    a1r, a1i, b1r, b1i = e1
    a2r, a2i, b2r, b2i = e2
    return (a2r * a1r - a2i * a1i,
            a2r * a1i + a2i * a1r,
            a2r * b1r - a2i * b1i + b2r,
            a2r * b1i + a2i * b1r + b2i)

def s5_branch(u, a_re, a_im, log_dt, b_re, b_im, c_re, c_im, d_skip, w_v, w_g):
    f32 = jnp.float32
    bsz, seq, _ = u.shape
    uf = u.astype(f32)
    ug = uf.reshape(bsz, seq, S5_GROUPS, S5_GROUP)
    dt = jnp.exp(log_dt.astype(f32))[:, None]
    ar = a_re.astype(f32)
    ai = a_im.astype(f32)
    mag = jnp.exp(ar * dt)
    lbar_re = mag * jnp.cos(ai * dt)
    lbar_im = mag * jnp.sin(ai * dt)
    den = ar * ar + ai * ai
    nr = lbar_re - 1.0
    ni = lbar_im
    f_re = (nr * ar + ni * ai) / den
    f_im = (ni * ar - nr * ai) / den
    br = b_re.astype(f32)
    bi = b_im.astype(f32)
    bbar_re = f_re[..., None] * br - f_im[..., None] * bi
    bbar_im = f_re[..., None] * bi + f_im[..., None] * br
    bu_re = jnp.einsum('blgc,gpc->blgp', ug, bbar_re)
    bu_im = jnp.einsum('blgc,gpc->blgp', ug, bbar_im)
    a_t_re = jnp.broadcast_to(lbar_re, bu_re.shape)
    a_t_im = jnp.broadcast_to(lbar_im, bu_im.shape)
    _, _, s_re, s_im = lax.associative_scan(
        _complex_affine_combine, (a_t_re, a_t_im, bu_re, bu_im), axis=1)
    y = (jnp.einsum('blgp,gcp->blgc', s_re, c_re.astype(f32))
         - jnp.einsum('blgp,gcp->blgc', s_im, c_im.astype(f32)))
    y = y.reshape(bsz, seq, S5_WIDTH) + d_skip.astype(f32) * uf
    y = jax.nn.gelu(y).astype(u.dtype)
    return (y @ w_v) * jax.nn.sigmoid(y @ w_g)

def rotary(t):
    seq, d = t.shape[1], t.shape[-1]
    inv = ROPE_BASE ** (-jnp.arange(0, d, 2, dtype=jnp.float32) / d)
    ang = jnp.arange(seq, dtype=jnp.float32)[:, None] * inv[None, :]
    cos = jnp.cos(ang)[None, :, None, :]
    sin = jnp.sin(ang)[None, :, None, :]
    t1, t2 = t[..., : d // 2], t[..., d // 2:]
    return jnp.concatenate([t1 * cos - t2 * sin, t1 * sin + t2 * cos], axis=-1)

def retention_branch(q, k, v, g, w_o):
    f32 = jnp.float32
    bsz, seq, _ = q.shape
    n_chunks = seq // RET_CHUNK
    q = rotary(q.astype(f32).reshape(bsz, seq, RET_HEADS, RET_QK_DIM))
    k = rotary(k.astype(f32).reshape(bsz, seq, RET_HEADS, RET_QK_DIM)) * (RET_QK_DIM ** -0.5)
    v = v.astype(f32).reshape(bsz, seq, RET_HEADS, RET_V_DIM)

    def to_chunks(t):
        return t.reshape(bsz, n_chunks, RET_CHUNK, RET_HEADS, t.shape[-1]).transpose(1, 0, 3, 2, 4)

    log_gamma = jnp.log(1.0 - 2.0 ** (-5.0 - jnp.arange(RET_HEADS, dtype=f32)))
    idx = jnp.arange(RET_CHUNK, dtype=f32)
    rel = idx[:, None] - idx[None, :]
    decay_inner = jnp.where(rel[None] >= 0,
                            jnp.exp(jnp.maximum(rel, 0.0)[None] * log_gamma[:, None, None]), 0.0)
    xi = jnp.exp((idx + 1.0)[None, :] * log_gamma[:, None])[None, :, :, None]
    zeta = jnp.exp((RET_CHUNK - 1.0 - idx)[None, :] * log_gamma[:, None])[None, :, :, None]
    gamma_c = jnp.exp(RET_CHUNK * log_gamma)[None, :, None, None]

    def step(state, qkv):
        qc, kc, vc = qkv
        scores = jnp.einsum('bhid,bhjd->bhij', qc, kc) * decay_inner
        out = (jnp.einsum('bhij,bhje->bhie', scores, vc)
               + jnp.einsum('bhid,bhde->bhie', qc, state) * xi)
        state = state * gamma_c + jnp.einsum('bhjd,bhje->bhde', kc * zeta, vc)
        return state, out

    state0 = jnp.zeros((bsz, RET_HEADS, RET_QK_DIM, RET_V_DIM), f32)
    _, o = lax.scan(step, state0, (to_chunks(q), to_chunks(k), to_chunks(v)))
    o = o.transpose(1, 0, 3, 2, 4).reshape(bsz, seq, RET_HEADS, RET_V_DIM)
    mean = jnp.mean(o, axis=-1, keepdims=True)
    var = jnp.mean(jnp.square(o - mean), axis=-1, keepdims=True)
    o = ((o - mean) * lax.rsqrt(var + GN_EPS)).reshape(bsz, seq, RET_V_WIDTH)
    o = (jax.nn.silu(g.astype(f32)) * o).astype(g.dtype)
    return o @ w_o

def cross_attention(h, m, wq, wk, wv, wo):
    bsz, seq, _ = h.shape
    mlen = m.shape[1]
    q = (h @ wq).reshape(bsz, seq, XATTN_HEADS, XATTN_HEAD_DIM).astype(jnp.float32)
    k = (m @ wk).reshape(bsz, mlen, XATTN_HEADS, XATTN_HEAD_DIM).astype(jnp.float32)
    v = (m @ wv).reshape(bsz, mlen, XATTN_HEADS, XATTN_HEAD_DIM).astype(jnp.float32)
    s = jnp.einsum('blhd,bmhd->bhlm', q, k) * (XATTN_HEAD_DIM ** -0.5)
    p = jax.nn.softmax(s, axis=-1)
    o = jnp.einsum('bhlm,bmhd->blhd', p, v).reshape(bsz, seq, D_MODEL).astype(h.dtype)
    return o @ wo

def setup_inputs(seed: int = 0) -> dict:
    key = jax.random.key(seed)
    ks = iter(jax.random.split(key, 40))
    f32 = jnp.float32

    def dense(shape, fan_in):
        return jax.random.normal(next(ks), shape, f32) * (fan_in ** -0.5)

    def gain(shape):
        return 1.0 + 0.02 * jax.random.normal(next(ks), shape, f32)

    L = DEPTH
    n_idx = jnp.arange(S5_STATE, dtype=f32)
    a_re = -0.5 + 0.01 * jax.random.normal(next(ks), (L, S5_GROUPS, S5_STATE), f32)
    a_im = jnp.pi * n_idx[None, None, :] + 0.01 * jax.random.normal(next(ks), (L, S5_GROUPS, S5_STATE), f32)
    log_dt = jax.random.uniform(next(ks), (L, S5_GROUPS), f32, math.log(DT_MIN), math.log(DT_MAX))
    return {
        "x": jax.random.normal(next(ks), (BATCH, SEQ, D_MODEL), f32),
        "mem": jax.random.normal(next(ks), (BATCH, MEM_LEN, D_MODEL), f32),
        "ffn1_norm": gain((L, D_MODEL)),
        "ffn1_w1": dense((L, D_MODEL, D_FF), D_MODEL),
        "ffn1_w3": dense((L, D_MODEL, D_FF), D_MODEL),
        "ffn1_w2": dense((L, D_FF, D_MODEL), D_FF),
        "mix_norm": gain((L, D_MODEL)),
        "w_in": dense((L, D_MODEL, N_IN), D_MODEL),
        "s5_a_re": a_re,
        "s5_a_im": a_im,
        "s5_log_dt": log_dt,
        "s5_b_re": dense((L, S5_GROUPS, S5_STATE, S5_GROUP), 2 * S5_GROUP),
        "s5_b_im": dense((L, S5_GROUPS, S5_STATE, S5_GROUP), 2 * S5_GROUP),
        "s5_c_re": dense((L, S5_GROUPS, S5_GROUP, S5_STATE), S5_STATE / 4.0),
        "s5_c_im": dense((L, S5_GROUPS, S5_GROUP, S5_STATE), S5_STATE / 4.0),
        "s5_d": jax.random.normal(next(ks), (L, S5_WIDTH), f32),
        "s5_glu_v": dense((L, S5_WIDTH, D_MODEL), S5_WIDTH),
        "s5_glu_g": dense((L, S5_WIDTH, D_MODEL), S5_WIDTH),
        "ret_w_o": dense((L, RET_V_WIDTH, D_MODEL), RET_V_WIDTH),
        "w_out": dense((L, D_MODEL, D_MODEL), D_MODEL),
        "xattn_norm": gain((L, D_MODEL)),
        "mem_norm": gain((L, D_MODEL)),
        "xattn_wq": dense((L, D_MODEL, D_MODEL), D_MODEL),
        "xattn_wk": dense((L, D_MODEL, D_MODEL), D_MODEL),
        "xattn_wv": dense((L, D_MODEL, D_MODEL), D_MODEL),
        "xattn_wo": dense((L, D_MODEL, D_MODEL), D_MODEL),
        "ffn2_norm": gain((L, D_MODEL)),
        "ffn2_w1": dense((L, D_MODEL, D_FF), D_MODEL),
        "ffn2_w3": dense((L, D_MODEL, D_FF), D_MODEL),
        "ffn2_w2": dense((L, D_FF, D_MODEL), D_FF),
        "final_norm": gain((D_MODEL,)),
    }

def reference(x, mem, ffn1_norm, ffn1_w1, ffn1_w3, ffn1_w2, mix_norm, w_in,
              s5_a_re, s5_a_im, s5_log_dt, s5_b_re, s5_b_im, s5_c_re, s5_c_im, s5_d,
              s5_glu_v, s5_glu_g, ret_w_o, w_out, xattn_norm, mem_norm,
              xattn_wq, xattn_wk, xattn_wv, xattn_wo,
              ffn2_norm, ffn2_w1, ffn2_w3, ffn2_w2, final_norm):
    splits = np.cumsum([S5_WIDTH, RET_QK_WIDTH, RET_QK_WIDTH, RET_V_WIDTH, RET_V_WIDTH, D_MODEL])
    h = x
    for l in range(DEPTH):
        h = h + 0.5 * swiglu(rms_norm(h, ffn1_norm[l]), ffn1_w1[l], ffn1_w3[l], ffn1_w2[l])
        u = rms_norm(h, mix_norm[l])
        proj = u @ w_in[l]
        u_s5, q, k, v, g_ret, gate_a, gate_b = jnp.split(proj, splits, axis=-1)
        y_a = s5_branch(u_s5, s5_a_re[l], s5_a_im[l], s5_log_dt[l], s5_b_re[l], s5_b_im[l],
                        s5_c_re[l], s5_c_im[l], s5_d[l], s5_glu_v[l], s5_glu_g[l])
        y_b = retention_branch(q, k, v, g_ret, ret_w_o[l])
        merged = jax.nn.sigmoid(gate_a) * y_a + jax.nn.sigmoid(gate_b) * y_b
        h = h + merged @ w_out[l]
        h = h + cross_attention(rms_norm(h, xattn_norm[l]), rms_norm(mem, mem_norm[l]),
                                xattn_wq[l], xattn_wk[l], xattn_wv[l], xattn_wo[l])
        h = h + 0.5 * swiglu(rms_norm(h, ffn2_norm[l]), ffn2_w1[l], ffn2_w3[l], ffn2_w2[l])
    return rms_norm(h, final_norm)


_drawn_inputs = setup_inputs


def setup_inputs(seed=0):
    import zlib

    import numpy as np

    out = dict(_drawn_inputs(seed))
    spreads = {}
    factors = {'ffn1_norm': 5.695,
     'mix_norm': 4.194,
     's5_a_re': 8.0,
     's5_b_re': 2.773,
     's5_b_im': 2.754,
     's5_c_re': 2.704,
     's5_c_im': 2.797,
     'xattn_norm': 8.0,
     'mem_norm': 8.0,
     'ffn2_norm': 7.788,
     'final_norm': 2.766}
    for name, (base, spread) in spreads.items():
        noise = np.random.default_rng([zlib.crc32(name.encode()), seed]).standard_normal(out[name].shape)
        drawn = base * np.exp(spread * noise) if base else spread * noise
        out[name] = __import__('jax').numpy.asarray(drawn.astype(out[name].dtype))
    for name, factor in factors.items():
        out[name] = (out[name] * factor).astype(out[name].dtype)
    return out
```

```python
import math
from contextlib import ExitStack

import concourse.bass as bass
from concourse import mybir

F32 = mybir.dt.float32
F32R = mybir.dt.float32r
ACT = mybir.ActivationFunctionType
ALU = mybir.AluOpType
AX_X = mybir.AxisListType.X

P = 128
SLOTS = 4
COLS = 512
D = 2048
SEQ = 256
KT = D // P
SUPER = 5632 // COLS
LAST = SUPER - 1
HEADS = 4
NBLK = D // COLS
QT = 1024 // P
PAIRS = 32
DOUBLES = 2 * HEADS
HALF = 16
RMS_EPS = 1e-6
GN_EPS = 1e-5
XSCALE = 512 ** -0.5
C_Q, C_V, C_G, C_GA, C_GB = 1024, 3072, 5120, 7168, 9216
G_FFN1, G_MIX, G_X, G_MEM, G_FFN2, G_D, VROWS = 0, 16, 32, 48, 64, 80, 88
ROUND = 1.5 * 2.0 ** 23
TWO_PI_A = 6.28125
TWO_PI_B = 4058 / 2.0 ** 21
TWO_PI_C = 2 * math.pi - TWO_PI_A - TWO_PI_B


def ds(start, size):
    return bass.ds(start, size)


def tok(t):
    return slice(t * P, (t + 1) * P)


def build(nc, x, mem, ffn1_norm, ffn1_w1, ffn1_w3, ffn1_w2, mix_norm, w_in, s5_a_re, s5_a_im,
          s5_log_dt, s5_b_re, s5_b_im, s5_c_re, s5_c_im, s5_d, s5_glu_v, s5_glu_g, ret_w_o, w_out,
          xattn_norm, mem_norm, xattn_wq, xattn_wk, xattn_wv, xattn_wo, ffn2_norm, ffn2_w1, ffn2_w3,
          ffn2_w2, final_norm, c_ident, c_rope, c_decay, c_parity, out):
    m_ffn1 = 0
    m_mix = m_ffn1 + 4 + 6 * LAST + 2
    m_heads = m_mix + 4
    m_merge = m_heads + 6 * HEADS
    m_wout = m_merge + 8 * NBLK
    m_xattn = m_wout + 2 * NBLK
    m_wo = m_xattn + 6 * HEADS
    m_ffn2 = m_wo + 2 * NBLK

    with ExitStack() as ctx:
        def sb(name, shape, dt=F32, where=ctx):
            return where.enter_context(nc.sbuf_tensor(name, shape, dt))

        def sem(name):
            return ctx.enter_context(nc.semaphore(name))

        h = sb("h", [P, 2, D])
        xt_hi = sb("xt_hi", [P, KT, SEQ], F32R)
        xt_lo = sb("xt_lo", [P, KT, SEQ], F32R)
        yt_hi = sb("yt_hi", [P, KT, SEQ], F32R)
        yt_lo = sb("yt_lo", [P, KT, SEQ], F32R)
        raw = sb("raw", [P, SLOTS, 2, COLS])
        w_hi = sb("w_hi", [P, SLOTS, 2, COLS], F32R)
        w_lo = sb("w_lo", [P, SLOTS, 2, COLS], F32R)
        nat = sb("nat", [P, 2, COLS])
        ident = sb("ident", [P, P])
        vecs = sb("vecs", [P, VROWS])
        sumsq = sb("sumsq", [P, 2, NBLK])
        meansq = sb("meansq", [P, 2])
        sumsq_mem = sb("sumsq_mem", [P, 2, NBLK])
        meansq_mem = sb("meansq_mem", [P, 2])
        mhalf = sb("mhalf", [P, 2])
        rstd = [sb(f"rstd{i}", [P, 2]) for i in range(5)]
        rstd_mem = sb("rstd_mem", [P, 2])
        mag = sb("mag", [P, PAIRS])

        with ExitStack() as plan:
            s5_tab = sb("s5_tab", [P, 4, PAIRS, HALF], F32, plan)
            b_t = sb("b_t", [P, 2, QT, P], F32, plan)
            c_t = sb("c_t", [P, 2, QT, P], F32, plan)
            u_t = sb("u_t", [P, QT, SEQ], F32, plan)
            with ExitStack() as part:
                gate = sb("gate", [P, 2, COLS], F32, part)
                hid = sb("hid", [P, 2, COLS], F32, part)
                ht_hi = sb("ht_hi", [P, 4, SEQ], F32R, part)
                ht_lo = sb("ht_lo", [P, 4, SEQ], F32R, part)
                junk = sb("junk", [P, COLS], F32, part)
                par = sb("par", [P, 26, PAIRS], F32, part)
                vrow = sb("vrow", [P, P], F32, part)
                prow = sb("prow", [P, P], F32, part)
                dt_row = sb("dt_row", [P, 2], F32, part)
                parity = sb("parity", [P, 2], F32, part)
                b_pad = sb("b_pad", [P, 2, PAIRS, 32], F32, part)
                c_pad = sb("c_pad", [P, 2, QT, P], F32, part)
            with ExitStack() as part:
                b_st = sb("b_st", [P, 2, P], F32, part)
                c_st = sb("c_st", [P, 2, P], F32, part)
                u_st = sb("u_st", [P, SEQ], F32, part)
                zb = sb("zb", [P, 2, 2, SEQ], F32, part)
                rot2 = sb("rot2", [P, 2, SEQ], F32, part)
                tab = sb("tab", [P, 2, 2, SEQ], F32, part)
                state = sb("state", [P, 2, 2, SEQ], F32, part)
                pool_tmp = sb("pool_tmp", [P, 2, SEQ], F32, part)
                on = sb("on", [P, 2, COLS], F32, part)
                qk_t = sb("qk_t", [P, 4, SEQ], F32, part)
                v_r = sb("v_r", [P, 2, COLS], F32, part)
                g_r = sb("g_r", [P, 2, COLS], F32, part)
                s_t = sb("s_t", [P, 2, SEQ], F32, part)
                rope = sb("rope", [P, 2, 2, P], F32, part)
                decay = sb("decay", [P, 384], F32, part)
                bstat = sb("bstat", [P, 2, 6], F32, part)
                mv = sb("mv", [P, 2, 2], F32, part)
                vare = sb("vare", [P, 2], F32, part)
                grstd = sb("grstd", [P, 2], F32, part)
        with ExitStack() as plan:
            sb("under_b_t", [P, 4, PAIRS, HALF], F32, plan)
            pow_tmp = sb("pow_tmp", [P, 2, PAIRS, HALF], F32, plan)
            sb("rest_of_b_t", [P, 2, PAIRS, HALF], F32, plan)
            b_raw = sb("b_raw", [P, 2, PAIRS, HALF], F32, plan)
            c_raw = sb("c_raw", [P, 2, QT, 64], F32, plan)
        with ExitStack() as plan:
            mt_hi = sb("mt_hi", [P, KT, SEQ], F32R, plan)
            mt_lo = sb("mt_lo", [P, KT, SEQ], F32R, plan)
            with ExitStack() as part:
                yb = sb("yb", [P, 2, COLS], F32, part)
                ga = sb("ga", [P, 2, COLS], F32, part)
                gb = sb("gb", [P, 2, COLS], F32, part)
                sg = sb("sg", [P, 2, COLS], F32, part)
                gl_hi = sb("gl_hi", [P, QT, SEQ], F32R, part)
                gl_lo = sb("gl_lo", [P, QT, SEQ], F32R, part)
                memb = sb("memb", [P, 2, COLS], F32, part)
                junk2 = sb("junk2", [P, COLS], F32, part)
            with ExitStack() as part:
                k_x = sb("k_x", [P, 4, SEQ], F32, part)
                q_x = sb("q_x", [P, 4, SEQ], F32, part)
                v_x = sb("v_x", [P, 2, COLS], F32, part)
                prob = sb("prob", [P, 2, SEQ], F32, part)
                prob_t = sb("prob_t", [P, 2, SEQ], F32, part)
                smax = sb("smax", [P, 2], F32, part)
                nmax = sb("nmax", [P, 2], F32, part)
                rowsum = sb("rowsum", [P, 2], F32, part)
                rinv = sb("rinv", [P, 2], F32, part)
        with ExitStack() as plan:
            gfin = sb("gfin", [P, D], F32, plan)

        acc = ctx.enter_context(nc.psum_tensor("acc", [P, 6, COLS], F32))
        tp = ctx.enter_context(nc.psum_tensor("tp", [P, 2, COLS], F32))
        tpk = tp[:, :, :].rearrange("p b (j s) -> p (b j) s", s=SEQ)
        s5_in = acc[:, 4, :].rearrange("p (r s) -> p r s", r=2)
        s5_out = acc[:, 5, 0:SEQ]

        raw_in = [sem(f"raw_in{i}") for i in range(SLOTS)]
        hi_done, lo_done, chunk_used = sem("hi_done"), sem("lo_done"), sem("chunk_used")
        tile0_done, v_tile0 = sem("tile0_done"), sem("v_tile0")
        ident_in, vec_in, par_in, bc_in, rope_in, decay_in, mem_in, gfin_in = (sem(n) for n in (
            "ident_in", "vec_in", "par_in", "bc_in", "rope_in", "decay_in", "mem_in", "gfin_in"))
        x_in = [sem(f"x_in{n}") for n in range(NBLK)]
        gain_in, gain_ps, gain_ready = sem("gain_in"), sem("gain_ps"), sem("gain_ready")
        dt_rows, vecs_ps, vecs_ready, par_ready, exp_dt, angles, trig = (
            sem(n) for n in ("dt_rows", "vecs_ps", "vecs_ready", "par_ready", "exp_dt", "angles",
                             "trig"))
        pads_ready, bc_ps, bc_ready = sem("pads_ready"), sem("bc_ps"), sem("bc_ready")
        blk_ps, blk_hi, blk_lo, sq_done, hb_ready = (sem(n) for n in (
            "blk_ps", "blk_hi", "blk_lo", "sq_done", "hb_ready"))
        ms_ready, rstd_ready = sem("ms_ready"), sem("rstd_ready")
        gate_ready, hid_ready, hid_ps, ht_h, ht_l, h_added = (
            [sem(f"{n}{f}") for f in range(2)]
            for n in ("gate_ready", "hid_ready", "hid_ps", "ht_h", "ht_l", "h_added"))
        u_nat, u_ps, u_ready, b_staged, c_staged, bu_done, x_free, tab_ready, z_ready, s_ready, \
            y_done, y_out, gelu_done, gl_h, gl_l = (sem(n) for n in (
                "u_nat", "u_ps", "u_ready", "b_staged", "c_staged", "bu_done", "x_free",
                "tab_ready", "z_ready", "s_ready", "y_done", "y_out", "gelu_done", "gl_h", "gl_l"))
        qk_nat, rot_ready, qk_ps, qk_ready, st_ps, st_ready, g_ready, v_ready, pv_ps, var_ready, \
            grstd_ready, og_ready, on_ready, on_ps, on_hi, on_lo = (sem(n) for n in (
                "qk_nat", "rot_ready", "qk_ps", "qk_ready", "st_ps", "st_ready", "g_ready",
                "v_ready", "pv_ps", "var_ready", "grstd_ready", "og_ready", "on_ready", "on_ps",
                "on_hi", "on_lo"))
        yb_ready, ga_ready, gb_ready, sg_ready, ybg_ready, va_ready, mg_ready, mg_ps, mg_hi, mg_lo = (
            sem(n) for n in ("yb_ready", "ga_ready", "gb_ready", "sg_ready", "ybg_ready",
                             "va_ready", "mg_ready", "mg_ps", "mg_hi", "mg_lo"))
        mem_ps, mem_hi, mem_lo, sqm_done, msm_ready, rstdm_ready = (sem(n) for n in (
            "mem_ps", "mem_hi", "mem_lo", "sqm_done", "msm_ready", "rstdm_ready"))
        kn_ready, kx_ps, kx_ready, qn_ready, qx_ps, qx_ready, sc_ps, nmax_ready, exp_ready, \
            prob_ready, pt_ps, pt_ready, vx_ready, xo_ps, xo_hi, xo_lo = (
                sem(n) for n in (
                    "kn_ready", "kx_ps", "kx_ready", "qn_ready", "qx_ps", "qx_ready", "sc_ps",
                    "nmax_ready", "exp_ready", "prob_ready", "pt_ps", "pt_ready", "vx_ready",
                    "xo_ps", "xo_hi", "xo_lo"))
        gfin_used, scaled_v, scaled_s, out_done = (
            sem(n) for n in ("gfin_used", "scaled_v", "scaled_s", "out_done"))

        ffn_parts = (
            (m_ffn1, ffn1_w1[0], ffn1_w3[0], ffn1_w2[0], 0),
            (m_ffn2, ffn2_w1[0], ffn2_w3[0], ffn2_w2[0], 3),
        )

        block = ctx.enter_context(nc.Block())

        @block.sync
        def _(sp):
            def fetch(m, c, src):
                if not (isinstance(m, int) and 4 * m + c < SLOTS):
                    sp.wait_ge(lo_done, 4 * m + c - SLOTS + 1)
                sp.dma_start(raw[:, c % SLOTS, :, :], src).then_inc(raw_in[c % SLOTS], 16)

            def piece(w, row, col):
                return w[ds(row, 2 * P), ds(col, COLS)].rearrange("(k p) n -> p k n", p=P)

            def column_block(m, c0, w, col, chunks=8):
                for c in range(chunks):
                    fetch(m, c0 + c, piece(w, 2 * P * c, col))

            def ffn(f):
                m0, w1, w3, w2, _ = ffn_parts[f]

                def down(m, c0, s):
                    for c in range(8):
                        fetch(m, c0 + c, piece(w2, s * COLS + 2 * P * (c % 2), COLS * (c // 2)))

                for c in range(8):
                    if f == 0 and 1 <= c < NBLK:
                        load_x(c)
                    fetch(m0, c, piece(w1, 2 * P * c, 0))
                column_block(m0, 8, w3, 0)
                with sp.Fori(1, LAST) as s:
                    m = m0 + 4 + 6 * (s - 1)
                    column_block(m, 0, w1, s * COLS)
                    down(m, 8, s - 1)
                    column_block(m, 16, w3, s * COLS)
                m = m0 + 4 + 6 * (LAST - 1)
                column_block(m, 0, w1, LAST * COLS)
                column_block(m, 8, w3, LAST * COLS)
                down(m, 16, LAST - 1)
                down(m + 6, 0, LAST)

            def load_x(n):
                sp.dma_start(h[:, :, n * COLS:(n + 1) * COLS],
                             x[0, :, n * COLS:(n + 1) * COLS].rearrange("(t p) d -> p t d", p=P)
                             ).then_inc(x_in[n], 16)

            sp.dma_start(ident[:, :], c_ident).then_inc(ident_in, 16)
            sp.dma_start(vrow[0:KT, :], ffn1_norm.rearrange("o (k p) -> (o k) p", p=P)
                         ).then_inc(gain_in, 16)
            load_x(0)
            ffn(0)

            w = w_in[0]
            column_block(m_mix, 0, w, 0)
            column_block(m_mix, 8, w, COLS)
            def head(hd, m, first):
                for c in range(8):
                    sp.wait_ge(lo_done, 4 * m + c - SLOTS + 1)
                    for b in range(2):
                        sp.dma_start(
                            raw[:, c % SLOTS, :, b * SEQ:(b + 1) * SEQ],
                            w[2 * P * c:2 * P * (c + 1), ds(C_Q + 1024 * b + hd * SEQ, SEQ)]
                            .rearrange("(k p) n -> p k n", p=P)).then_inc(raw_in[c % SLOTS], 16)
                    if c == 4:
                        if first:
                            sp.wait_ge(bc_ps, 8)
                            sp.dma_start(rope[:, :, :, :], c_rope).then_inc(rope_in, 16)
                        else:
                            sp.wait_ge(st_ready, hd)
                        sp.dma_start(decay[:, :], c_decay[ds(hd * P, P), :]).then_inc(decay_in, 16)
                column_block(m, 8, w, C_G + hd * COLS)
                column_block(m, 16, w, C_V + hd * COLS)

            head(0, m_heads, True)
            with sp.Fori(1, HEADS) as hd:
                head(hd, m_heads + 6 * hd, False)

            def merge(n, m, first):
                if first:
                    column_block(m, 0, w, C_GA + n * COLS)
                    column_block(m, 8, ret_w_o[0], n * COLS)
                else:
                    column_block(m, 0, ret_w_o[0], n * COLS)
                    column_block(m, 8, w, C_GA + n * COLS)
                column_block(m, 16, w, C_GB + n * COLS)
                column_block(m, 24, s5_glu_v[0], n * COLS, 4)
                column_block(m, 28, s5_glu_g[0], n * COLS, 4)

            merge(0, m_merge, True)
            with sp.Fori(1, NBLK) as n:
                merge(n, m_merge + 8 * n, False)
            with sp.Fori(0, NBLK) as n:
                column_block(m_wout + 2 * n, 0, w_out[0], n * COLS)
            with sp.Fori(0, HEADS) as hd:
                m = m_xattn + 6 * hd
                column_block(m, 0, xattn_wk[0], hd * COLS)
                column_block(m, 8, xattn_wq[0], hd * COLS)
                column_block(m, 16, xattn_wv[0], hd * COLS)
            with sp.Fori(0, NBLK) as n:
                column_block(m_wo + 2 * n, 0, xattn_wo[0], n * COLS)
            ffn(1)
            for t, b0, b1, scaled, count in ((0, 0, 2, scaled_v, 2), (1, 0, 3, scaled_s, 1),
                                             (0, 2, 4, scaled_v, 4), (1, 3, 4, scaled_v, 5)):
                sp.wait_ge(scaled, count)
                sp.dma_start(out[0, tok(t), b0 * COLS:b1 * COLS],
                             h[:, t, b0 * COLS:b1 * COLS]).then_inc(out_done, 16)
            sp.wait_ge(out_done, 16 * 4)

        @block.scalar
        def _(act):
            def split_hi(m, c, doubles=0):
                act.wait_ge(raw_in[c % SLOTS], 16 * (m + c // SLOTS + 1 + doubles))
                if not (isinstance(m, int) and 4 * m + c < SLOTS):
                    act.wait_ge(chunk_used, 4 * m + c - SLOTS + 1)
                act.activation(w_hi[:, c % SLOTS, :, :], raw[:, c % SLOTS, :, :],
                               ACT.Copy).then_inc(hi_done, 1)

            def evacuate(dst, pair, scale, done, func=ACT.Copy):
                for t in range(2):
                    i = act.activation(dst[:, t, :], acc[:, pair + t, :], func,
                                       scale=1.0 if scale is None else scale[:, t:t + 1])
                i.then_inc(done, 1)

            def block_split(b, gain, kt):
                act.wait_ge(blk_ps, b + 1)
                for j in range(4):
                    i = act.activation(xt_hi[:, ds(kt + j, 1), :], tpk[:, j:j + 1, :], ACT.Copy,
                                       scale=vecs[:, ds(gain + kt + j, 1)])
                i.then_inc(blk_hi, 1)

            def block_squares(src, n, unused):
                for t in range(2):
                    act.drain()
                    i = act.activation(unused[:, :], src[:, t, :], ACT.Square,
                                       accum_out=sumsq[:, t, ds(n, 1)])
                i.then_inc(sq_done, 1)

            def block_hi(b, gain, kt, src, n):
                block_split(b, gain, kt)
                block_squares(src, n, junk if b < 8 else junk2)

            def h_cols(n):
                return h[:, :, n * COLS:(n + 1) * COLS]

            def ffn(f):
                m0 = ffn_parts[f][0]
                scale = rstd[ffn_parts[f][4]]

                def silu_gate(m, s):
                    act.wait_ge(chunk_used, 4 * m + 8)
                    evacuate(gate, 0, scale, gate_ready[f], ACT.Silu)

                def hidden_hi(s, dst=ht_hi[:, :, :]):
                    act.wait_ge(hid_ps[f], s + 1)
                    act.activation(dst, tpk, ACT.Copy).then_inc(ht_h[f], 1)

                doubles = DOUBLES * f
                for c in range(16):
                    split_hi(m0, c, doubles)
                    if f == 0 and c in (0, 3, 5):
                        n = (c + 2) // 2
                        block_split(n, G_FFN1, 4 * n)
                    if f == 0 and 5 < c < 10:
                        block_squares(h_cols(c - 6), c - 6, junk)
                    if f == 0 and c == 11:
                        vectors_and_parameters()
                    if f == 0 and c == 13:
                        s5_step_size()
                    if f == 1 and c == 4:
                        block_hi(15, G_FFN2, 12, nat, 3)
                    if f == 1 and c == 6:
                        copy_h(3, 12)
                    if c == (12 if f == 0 else 10):
                        act.wait_ge(rstd_ready, 1 if f == 0 else 4)
                        silu_gate(m0, 0)
                with act.Fori(1, LAST) as s:
                    m = m0 + 4 + 6 * (s - 1)
                    for c in range(24):
                        split_hi(m, c, doubles)
                        if c == 6:
                            hidden_hi(s - 1)
                        if c == 10:
                            silu_gate(m, s)
                m = m0 + 4 + 6 * (LAST - 1)
                for c in range(24):
                    split_hi(m, c, doubles)
                    if c == 6:
                        hidden_hi(LAST - 1)
                    if c == 10:
                        silu_gate(m, LAST)
                    if f == 0 and c == 14:
                        s5_trig()
                    if c == 22:
                        hidden_hi(LAST, yt_hi[:, 0:4, :])
                m += 6
                for c in range(8):
                    split_hi(m, c, doubles)
                    if f == 0 and c == 6:
                        block_hi(4, G_MIX, 0, h_cols(0), 0)
                    if f == 1 and c in (5, 7):
                        n = (c - 5) // 2
                        act.wait_ge(h_added[1], 4 * LAST + n + 1)
                        block_squares(h_cols(n), n, junk)

            def vectors_and_parameters():
                act.wait_ge(vecs_ps, 1)
                act.activation(vecs[:, KT:VROWS], tp[:, 0, KT:VROWS], ACT.Copy)
                act.activation(par[:, 0:3, :].rearrange("p a b -> p (a b)"), tp[:, 1, 0:96],
                               ACT.Copy).then_inc(par_ready, 1)

            def s5_step_size():
                act.wait_ge(par_ready, 1)
                act.activation(par[:, 3, :], par[:, 2, :], ACT.Exp).then_inc(exp_dt, 1)

            def s5_trig():
                act.wait_ge(angles, 1)
                act.activation(mag[:, :], par[:, 4, :], ACT.Exp)
                act.activation(par[:, 9, :], par[:, 7, :], ACT.Sin, scale=0.5)
                act.activation(par[:, 10, :], par[:, 7, :], ACT.Sin).then_inc(trig, 1)

            def copy_h(n, b0):
                act.wait_ge(hb_ready, 2 * (b0 - 8 + n) + 2)
                act.activation(h[:, :, ds(n * COLS, COLS)], nat[:, :, :], ACT.Copy)

            act.wait_ge(gain_ps, 1)
            act.activation(vecs[:, 0:KT], acc[:, 4, 0:KT], ACT.Copy).then_inc(gain_ready, 1)
            act.wait_ge(gain_ready, 1)
            block_split(0, G_FFN1, 0)
            ffn(0)

            for c in range(16):
                split_hi(m_mix, c)
                if c in (1, 3, 5):
                    n = (c + 1) // 2
                    block_hi(4 + n, G_MIX, 4 * n, h_cols(n), n)
                if 5 <= c < 13:
                    g = c - 5
                    act.wait_ge(bc_ps, g + 1)
                    dst = (b_t if g < 4 else c_t)[:, (g // 2) % 2, 4 * (g % 2):4 * (g % 2) + 4, :]
                    act.activation(dst.rearrange("p a b -> p (a b)"), acc[:, 4 + g % 2, :],
                                   ACT.Copy).then_inc(bc_ready, 1)
                if c == 10:
                    act.wait_ge(rstd_ready, 2)
                    act.wait_ge(chunk_used, 4 * m_mix + 8)
                    evacuate(nat, 2, rstd[1], u_nat)

            def values(hd, m):
                for t in range(2):
                    act.wait_ge(chunk_used if t else v_tile0, 4 * m if t else hd + 1)
                    act.activation(v_r[:, t, :], acc[:, 2 + t, :], ACT.Copy,
                                   scale=rstd[1][:, t:t + 1]).then_inc(v_ready, 1)

            def stage_b(q):
                act.activation(b_st[:, :, :], b_t[:, :, ds(q, 1), :].rearrange("p r o s -> p r (o s)"),
                               ACT.Copy)
                act.activation(u_st[:, :], u_t[:, ds(q, 1), :].rearrange("p o s -> p (o s)"),
                               ACT.Copy).then_inc(b_staged, 1)

            def stage_c(q):
                act.activation(c_st[:, :, :], c_t[:, :, ds(q, 1), :].rearrange("p r o s -> p r (o s)"),
                               ACT.Copy).then_inc(c_staged, 1)

            def group_scale(hd):
                act.wait_ge(grstd_ready, hd + 1)
                act.wait_ge(og_ready, hd + 1)
                for t in range(2):
                    i = act.activation(on[:, t, :], on[:, t, :], ACT.Copy, scale=grstd[:, t:t + 1])
                i.then_inc(on_ready, 1)

            def retention_hi(hd):
                act.wait_ge(on_ps, hd + 1)
                act.activation(yt_hi[:, ds(4 * hd, 4), :], tpk, ACT.Copy).then_inc(on_hi, 1)

            def head(hd, m, first):
                for c in range(24):
                    split_hi(m, c, 2 * hd + min(c // SLOTS + 1, 2))
                    if c == 0:
                        if first:
                            act.wait_ge(bc_ready, 8)
                            act.wait_ge(u_ready, 1)
                        else:
                            act.wait_ge(bu_done, 8 * hd)
                        stage_b(2 * hd)
                    if c == 1 and not first:
                        values(hd - 1, m)
                    if c == 2 and first:
                        act.wait_ge(chunk_used, 4 * m)
                        act.wait_ge(u_ps, 1)
                        evacuate(nat, 0, rstd[1], u_nat)
                    if c == 6:
                        if not first:
                            act.wait_ge(y_done, 8 * hd)
                        stage_c(2 * hd)
                        if not first:
                            group_scale(hd - 1)
                    if c == 9 and not first:
                        retention_hi(hd - 1)
                    if c == 10:
                        act.wait_ge(chunk_used, 4 * m + 8)
                        if first:
                            act.wait_ge(u_ps, 2)
                        evacuate(nat, 2, rstd[1], qk_nat)
                    if c == 12:
                        act.wait_ge(bu_done, 8 * hd + 4)
                        stage_b(2 * hd + 1)
                    if c == 17:
                        act.wait_ge(qk_ps, hd + 1)
                        act.activation(qk_t[:, :, :], tpk, ACT.Copy).then_inc(qk_ready, 1)
                    if c == 18:
                        act.wait_ge(y_done, 8 * hd + 4)
                        stage_c(2 * hd + 1)
                        act.wait_ge(chunk_used, 4 * m + 16)
                        evacuate(g_r, 0, rstd[1], g_ready, ACT.Silu)

            head(0, m_heads, True)
            with act.Fori(1, HEADS) as hd:
                head(hd, m_heads + 6 * hd, False)

            def glu_gate(n, m):
                act.wait_ge(chunk_used, 4 * m)
                evacuate(sg, 4, None, sg_ready, ACT.Sigmoid)

            def merged_hi(n):
                act.wait_ge(mg_ps, n + 1)
                act.activation(mt_hi[:, ds(4 * n, 4), :], tpk, ACT.Copy).then_inc(mg_hi, 1)

            def merge(n, m, first):
                for c in range(32):
                    split_hi(m, c, DOUBLES)
                    if c == 1:
                        if first:
                            values(HEADS - 1, m)
                        else:
                            glu_gate(n - 1, m)
                    if first and c == 6:
                        group_scale(HEADS - 1)
                    if first and c == 9:
                        retention_hi(HEADS - 1)
                    if not first and c == 5:
                        merged_hi(n - 1)
                    if c == (10 if first else 18):
                        act.wait_ge(chunk_used, 4 * m + c - 2)
                        evacuate(ga, 0 if first else 2, rstd[1], ga_ready, ACT.Sigmoid)
                    if first and c == 12:
                        act.wait_ge(y_out, QT)
                        act.activation(u_t[:, :, :], u_t[:, :, :],
                                       ACT.Gelu_apprx_tanh).then_inc(gelu_done, 1)
                    if first and c == 13:
                        act.wait_ge(gelu_done, 1)
                        act.activation(gl_hi[:, :, :], u_t[:, :, :], ACT.Copy).then_inc(gl_h, 1)
                    if c == (18 if first else 10):
                        act.wait_ge(chunk_used, 4 * m + c - 2)
                        evacuate(yb, 2 if first else 0, None, yb_ready)
                    if c == 26:
                        act.wait_ge(chunk_used, 4 * m + 24)
                        evacuate(gb, 0, rstd[1], gb_ready, ACT.Sigmoid)

            merge(0, m_merge, True)
            with act.Fori(1, NBLK) as n:
                merge(n, m_merge + 8 * n, False)

            def memory_hi(n):
                act.wait_ge(mem_ps, n + 1)
                for j in range(4):
                    i = act.activation(yt_hi[:, ds(4 * n + j, 1), :], tpk[:, j:j + 1, :],
                                       ACT.Copy, scale=vecs[:, ds(G_MEM + 4 * n + j, 1)])
                i.then_inc(mem_hi, 1)
                for t in range(2):
                    act.drain()
                    i = act.activation(junk2[:, :], memb[:, t, :], ACT.Square,
                                       accum_out=sumsq_mem[:, t, ds(n, 1)])
                i.then_inc(sqm_done, 1)

            def mixer_projection(n, m, first):
                for c in range(8):
                    split_hi(m, c, DOUBLES)
                    if first and c == 1:
                        glu_gate(NBLK - 1, m)
                    if first and c == 5:
                        merged_hi(NBLK - 1)
                    if not first and c == 2:
                        memory_hi(n - 1)
                    if not first and c == 4:
                        copy_h(n - 1, 8)
                    if not first and c == 6:
                        block_hi(8 + n - 1, G_X, 4 * (n - 1), nat, n - 1)

            mixer_projection(0, m_wout, True)
            with act.Fori(1, NBLK) as n:
                mixer_projection(n, m_wout + 2 * n, False)

            def attn_values(hd, m):
                act.wait_ge(chunk_used, 4 * m)
                evacuate(v_x, 4, rstd_mem, vx_ready)

            def attn_hi(hd):
                act.wait_ge(xo_ps, hd + 1)
                act.activation(mt_hi[:, ds(4 * hd, 4), :], tpk, ACT.Copy).then_inc(xo_hi, 1)

            def attn_head(hd, m, first):
                for c in range(24):
                    split_hi(m, c, DOUBLES)
                    if c == 1 and not first:
                        attn_values(hd - 1, m)
                    if c == 2 and first:
                        memory_hi(NBLK - 1)
                    if c == 4 and not first:
                        attn_hi(hd - 1)
                    if c == 4 and first:
                        copy_h(3, 8)
                    if c == 6 and first:
                        block_hi(11, G_X, 12, nat, 3)
                    if c == 10:
                        act.wait_ge(chunk_used, 4 * m + 8)
                        act.wait_ge(rstdm_ready, 1)
                        evacuate(nat, 0, rstd_mem, kn_ready)
                    if c == 13:
                        act.wait_ge(kx_ps, hd + 1)
                        act.activation(k_x[:, :, :], tpk, ACT.Copy).then_inc(kx_ready, 1)
                    if c == 17:
                        act.wait_ge(chunk_used, 4 * m + 16)
                        act.wait_ge(rstd_ready, 3)
                        evacuate(nat, 2, rstd[2], qn_ready)
                    if c == 19:
                        act.wait_ge(qx_ps, hd + 1)
                        act.activation(q_x[:, :, :], tpk, ACT.Copy).then_inc(qx_ready, 1)
                    if c == 21:
                        act.wait_ge(nmax_ready, hd + 1)
                        for t in range(2):
                            i = act.activation(prob[:, t, :], tpk[:, t, :], ACT.Exp, scale=XSCALE,
                                               bias=nmax[:, t:t + 1], accum_out=rowsum[:, t:t + 1])
                        i.then_inc(exp_ready, 1)
                    if c == 23:
                        act.wait_ge(pt_ps, hd + 1)
                        act.activation(prob_t[:, :, :].rearrange("p a b -> p (a b)"), tp[:, 1, :],
                                       ACT.Copy).then_inc(pt_ready, 1)

            attn_head(0, m_xattn, True)
            with act.Fori(1, HEADS) as hd:
                attn_head(hd, m_xattn + 6 * hd, False)

            def attn_projection(n, m, first):
                for c in range(8):
                    split_hi(m, c, DOUBLES)
                    if first and c == 1:
                        attn_values(HEADS - 1, m)
                    if first and c == 4:
                        attn_hi(HEADS - 1)
                    if not first and c == 3:
                        copy_h(n - 1, 12)
                    if not first and c == 4:
                        block_hi(12 + n - 1, G_FFN2, 4 * (n - 1), nat, n - 1)

            attn_projection(0, m_wo, True)
            with act.Fori(1, NBLK) as n:
                attn_projection(n, m_wo + 2 * n, False)
            ffn(1)
            act.wait_ge(h_added[1], 4 * LAST + 3)
            block_squares(h_cols(2), 2, junk)
            for t in range(2):
                act.wait_ge(h_added[1], 4 * LAST + 4 + t)
                if t:
                    act.drain()
                i = act.activation(junk[:, :], h[:, t, 3 * COLS:], ACT.Square,
                                   accum_out=sumsq[:, t, 3:4])
            i.then_inc(sq_done, 1)
            act.wait_ge(gfin_used, 3)
            act.wait_ge(rstd_ready, 5)
            act.activation(h[:, 1, 0:3 * COLS], h[:, 1, 0:3 * COLS], ACT.Copy,
                           scale=rstd[4][:, 1:2]).then_inc(scaled_s, 1)

        @block.vector
        def _(dve):
            def split_lo(m, c):
                dve.wait_ge(hi_done, 4 * m + c + 1)
                dve.tensor_tensor(w_lo[:, c % SLOTS, :, :], raw[:, c % SLOTS, :, :],
                                  w_hi[:, c % SLOTS, :, :].bitcast(F32),
                                  ALU.subtract).then_inc(lo_done, 1)

            def block_lo(b, gain, kt):
                dve.wait_ge(blk_hi, b + 1)
                for j in range(4):
                    i = dve.scalar_tensor_tensor(
                        out=xt_lo[:, ds(kt + j, 1), :], in0=tpk[:, j:j + 1, :],
                        scalar=vecs[:, ds(gain + kt + j, 1)],
                        in1=xt_hi[:, ds(kt + j, 1), :].bitcast(F32), op0=ALU.mult, op1=ALU.subtract)
                i.then_inc(blk_lo, 1)

            def mean_square(sums, mean, ready, sums_done, count):
                dve.wait_ge(sums_done, count)
                dve.tensor_reduce(mean[:, :], sums[:, :, :], AX_X, ALU.add)
                dve.drain()
                dve.tensor_scalar(mean[:, :], mean[:, :], 1.0 / D, RMS_EPS, ALU.mult,
                                  ALU.add).then_inc(ready, 1)

            def lo_of(dst_hi, dst_lo, done_hi, count, done):
                dve.wait_ge(done_hi, count)
                dve.tensor_tensor(dst_lo, tpk, dst_hi.bitcast(F32), ALU.subtract).then_inc(done, 1)

            def ffn(f):
                m0 = ffn_parts[f][0]
                scale = rstd[ffn_parts[f][4]]

                def hidden(m, s):
                    dve.wait_ge(chunk_used, 4 * m)
                    dve.wait_ge(gate_ready[f], s + 1)
                    for t in range(2):
                        i = dve.scalar_tensor_tensor(out=hid[:, t, :], in0=acc[:, 2 + t, :],
                                                     scalar=scale[:, t:t + 1], in1=gate[:, t, :],
                                                     op0=ALU.mult, op1=ALU.mult)
                    i.then_inc(hid_ready[f], 1)

                def add_half(m, c, n, pairs=(4, 2, 4, 0)):
                    dve.wait_ge(chunk_used, 4 * m + c + 1)
                    pair = pairs[n]
                    for t in range(2):
                        hb = h[:, t, n * COLS:(n + 1) * COLS]
                        i = dve.scalar_tensor_tensor(out=hb, in0=acc[:, pair + t, :], scalar=0.5,
                                                     in1=hb, op0=ALU.mult, op1=ALU.add)
                    i.then_inc(h_added[f], 1)

                for c in range(16):
                    split_lo(m0, c)
                    if f == 0 and c in (0, 3, 5):
                        n = (c + 2) // 2
                        block_lo(n, G_FFN1, 4 * n)
                    if f == 0 and c == 4:
                        step_rows()
                    if f == 0 and c == 10:
                        mean_square(sumsq, meansq, ms_ready, sq_done, 4)
                    if f == 1 and c == 1:
                        add_block(NBLK - 1, m0, 8)
                    if f == 1 and c == 4:
                        block_lo(15, G_FFN2, 12)
                    if f == 1 and c == 5:
                        mean_square(sumsq, meansq, ms_ready, sq_done, 16)
                with dve.Fori(1, LAST) as s:
                    m = m0 + 4 + 6 * (s - 1)
                    for c in range(24):
                        split_lo(m, c)
                        if c == 3:
                            hidden(m, s - 1)
                        if c == 6:
                            lo_of(ht_hi[:, :, :], ht_lo[:, :, :], ht_h[f], s, ht_l[f])
                        if c in (12, 14, 16, 18):
                            add_half(m, c - 3, (c - 12) // 2)
                m = m0 + 4 + 6 * (LAST - 1)
                other_pairs = (4, 0, 4, 2)
                for c in range(24):
                    split_lo(m, c)
                    if c == 3:
                        hidden(m, LAST - 1)
                    if c == 6:
                        lo_of(ht_hi[:, :, :], ht_lo[:, :, :], ht_h[f], LAST, ht_l[f])
                    if c == 18:
                        hidden(m + 4, LAST)
                    if c in (20, 21):
                        add_half(m, 17 + 2 * (c - 20), c - 20, other_pairs)
                    if c == 22:
                        lo_of(yt_hi[:, 0:4, :], yt_lo[:, 0:4, :], ht_h[f], SUPER, ht_l[f])
                for c in range(8):
                    split_lo(m + 6, c)
                    if c in (0, 1):
                        add_half(m, 21 + 2 * c, 2 + c, other_pairs)
                    if c in (3, 5, 7):
                        add_half(m + 6, c - 2, (c - 3) // 2)
                    if f == 0 and c == 6:
                        block_lo(4, G_MIX, 0)
                    if f == 1 and c in (6, 7):
                        apply_gain(c - 6)
                return add_half

            def apply_gain(n):
                if n == 0:
                    dve.wait_ge(gfin_in, 16)
                dve.wait_ge(sq_done, 16 + n + 1)
                g = gfin[:, n * COLS:(n + 1) * COLS].unsqueeze(1).broadcast_to([P, 2, COLS])
                hb = h[:, :, n * COLS:(n + 1) * COLS]
                dve.tensor_tensor(hb, hb, g, ALU.mult).then_inc(gfin_used, 1)

            def step_rows():
                dve.wait_ge(par_in, 48)
                dve.tensor_copy(prow[64:96, :].rearrange("p (g s) -> p g s", g=2),
                                dt_row[64:96, :].unsqueeze(2).broadcast_to([PAIRS, 2, 64])
                                ).then_inc(dt_rows, 1)

            dve.memset(mhalf[:, :], -0.5)
            block_lo(0, G_FFN1, 0)
            add_half = ffn(0)

            m_tail = m_mix - 2
            for c in range(16):
                split_lo(m_mix, c)
                if c == 1:
                    add_half(m_tail, 7, 3)
                if c in (1, 3, 5):
                    block_lo(4 + (c + 1) // 2, G_MIX, 2 * (c + 1))
                if c == 6:
                    mean_square(sumsq, meansq, ms_ready, sq_done, 8)
                if c == 14:
                    dve.wait_ge(u_ps, 1)
                    dve.tensor_copy(u_t[:, 0:4, :], tpk).then_inc(u_ready, 1)

            def rotate_and_scan(hd, p, first):
                buf = p % 2
                dve.wait_ge(bu_done, 8 * hd + p + 1)
                dve.wait_ge(tab_ready, 8 * hd + p + 1)
                if not (first and p in (0, 1)):
                    dve.wait_ge(s_ready, 8 * hd + p - 1)
                z = zb[:, buf, :, :]
                dve.tensor_tensor(z, s5_in, tab[:, buf, 0:1, :].broadcast_to([P, 2, SEQ]), ALU.mult)
                dve.tensor_tensor(rot2[:, :, :], s5_in, tab[:, buf, 1:2, :].broadcast_to([P, 2, SEQ]),
                                  ALU.mult).then_inc(x_free, 1)
                dve.drain()
                dve.tensor_tensor(zb[:, buf, 0, :], zb[:, buf, 0, :], rot2[:, 1, :], ALU.add)
                dve.tensor_tensor(zb[:, buf, 1, :], zb[:, buf, 1, :], rot2[:, 0, :], ALU.subtract)
                dve.drain()
                r = mag[:, ds(8 * hd + p, 1)].broadcast_to([P, SEQ])
                for part in range(2):
                    i = dve.tensor_tensor_scan(zb[:, buf, part, :], r, zb[:, buf, part, :], 0.0,
                                               ALU.mult, ALU.add)
                i.then_inc(z_ready, 1)

            def add_skip(q):
                dve.wait_ge(y_done, 4 * q + 4)
                u = u_t[:, ds(q, 1), :].rearrange("p o s -> p (o s)")
                dve.scalar_tensor_tensor(out=u, in0=u, scalar=vecs[:, ds(G_D + q, 1)], in1=s5_out,
                                         op0=ALU.mult, op1=ALU.add).then_inc(y_out, 1)

            def group_stats(hd):
                dve.wait_ge(pv_ps, hd + 1)
                for t in range(2):
                    dve.bn_stats(bstat[:, t, :], tp[:, t, :])
                dve.drain()
                for t in range(2):
                    dve.bn_aggr(mv[:, t, :], bstat[:, t, :])
                dve.drain()
                dve.tensor_scalar(vare[:, :], mv[:, :, 1], GN_EPS, None,
                                  ALU.add).then_inc(var_ready, 1)

            def group_gate(hd):
                dve.wait_ge(g_ready, hd + 1)
                for t in range(2):
                    i = dve.scalar_tensor_tensor(out=on[:, t, :], in0=tp[:, t, :],
                                                 scalar=mv[:, t, 0:1], in1=g_r[:, t, :],
                                                 op0=ALU.subtract, op1=ALU.mult)
                i.then_inc(og_ready, 1)

            def rotary(hd, t):
                dve.wait_ge(qk_nat, hd + 1)
                src = nat[:, t, :].rearrange("p (a d) -> p a d", d=P)
                for s in range(2):
                    dve.tensor_tensor(on[:, s, :].rearrange("p (a d) -> p a d", d=P), src,
                                      rope[:, t, s:s + 1, :].broadcast_to([P, 4, P]), ALU.mult)
                dve.drain()
                dst = nat[:, t, :].rearrange("p (a f d) -> p a f d", a=2, f=2)
                cos = on[:, 0, :].rearrange("p (a f d) -> p a f d", a=2, f=2)
                sin = on[:, 1, :].rearrange("p (a f d) -> p a f d", a=2, f=2)
                dve.tensor_tensor(dst[:, :, 0, :], cos[:, :, 0, :], sin[:, :, 1, :], ALU.subtract)
                dve.tensor_tensor(dst[:, :, 1, :], cos[:, :, 1, :], sin[:, :, 0, :],
                                  ALU.add).then_inc(rot_ready, 1)

            def retention_lo(hd):
                lo_of(yt_hi[:, ds(4 * hd, 4), :], yt_lo[:, ds(4 * hd, 4), :], on_hi, hd + 1, on_lo)

            def head(hd, m, first):
                for c in range(24):
                    split_lo(m, c)
                    if c % 3 == 0 and not (first and c == 0):
                        rotate_and_scan(hd, c // 3 - 1, first)
                    if not first and c == 2:
                        group_stats(hd - 1)
                    if not first and c == 4:
                        group_gate(hd - 1)
                    if not first and c == 5:
                        add_skip(2 * hd - 1)
                    if c == 6 and first:
                        dve.wait_ge(u_ps, 2)
                        dve.tensor_copy(u_t[:, 4:8, :], tpk).then_inc(u_ready, 1)
                    if c == 10 and not first:
                        retention_lo(hd - 1)
                    if c == 11:
                        if first:
                            dve.wait_ge(rope_in, 16)
                        rotary(hd, 0)
                    if c == 13:
                        dve.drain()
                        rotary(hd, 1)
                    if c == 17:
                        add_skip(2 * hd)
                    if c == 20:
                        dve.wait_ge(st_ps, hd + 1)
                        dve.wait_ge(decay_in, 16 * (hd + 1))
                        dve.tensor_tensor(s_t[:, 0, :], tp[:, 0, 0:SEQ], decay[:, 0:SEQ], ALU.mult)
                        dve.tensor_tensor(s_t[:, 1, P:SEQ], tp[:, 0, 384:512], decay[:, SEQ:384],
                                          ALU.mult).then_inc(st_ready, 1)

            head(0, m_heads, True)
            with dve.Fori(1, HEADS) as hd:
                head(hd, m_heads + 6 * hd, False)

            def add_branches(n):
                dve.wait_ge(sg_ready, n + 1)
                dve.tensor_tensor(ga[:, :, :], ga[:, :, :], sg[:, :, :], ALU.mult)
                dve.drain()
                dve.tensor_tensor(yb[:, :, :], yb[:, :, :], ga[:, :, :], ALU.add).then_inc(mg_ready, 1)

            def merged_lo(n):
                lo_of(mt_hi[:, ds(4 * n, 4), :], mt_lo[:, ds(4 * n, 4), :], mg_hi, n + 1, mg_lo)

            def merge(n, m, first):
                for c in range(32):
                    split_lo(m, c)
                    if first and c == 0:
                        rotate_and_scan(HEADS, -1, False)
                    if first and c == 2:
                        group_stats(HEADS - 1)
                    if first and c == 4:
                        group_gate(HEADS - 1)
                    if first and c == 6:
                        add_skip(QT - 1)
                    if first and c == 10:
                        retention_lo(HEADS - 1)
                    if not first and c == 2:
                        add_branches(n - 1)
                    if not first and c == 5:
                        merged_lo(n - 1)
                    if first and c == 16:
                        dve.wait_ge(gl_h, 1)
                        dve.tensor_tensor(gl_lo[:, :, :], u_t[:, :, :], gl_hi[:, :, :].bitcast(F32),
                                          ALU.subtract).then_inc(gl_l, 1)
                    if c == 28:
                        dve.wait_ge(gb_ready, n + 1)
                        dve.tensor_tensor(yb[:, :, :], yb[:, :, :], gb[:, :, :], ALU.mult)
                    if c == 30:
                        dve.wait_ge(chunk_used, 4 * m + 28)
                        for t in range(2):
                            i = dve.tensor_tensor(ga[:, t, :], acc[:, 2 + t, :], ga[:, t, :], ALU.mult)
                        i.then_inc(va_ready, 1)

            merge(0, m_merge, True)
            with dve.Fori(1, NBLK) as n:
                merge(n, m_merge + 8 * n, False)

            def add_block(n, m, b0):
                for t in range(2):
                    if t == 0:
                        dve.wait_ge(tile0_done, b0 + n + 1 - 4)
                    else:
                        dve.wait_ge(chunk_used, 4 * m)
                    dve.tensor_tensor(nat[:, t, :], acc[:, 2 + t, :],
                                      h[:, t, ds(n * COLS, COLS)], ALU.add).then_inc(hb_ready, 1)

            def memory_lo(n):
                dve.wait_ge(mem_hi, n + 1)
                for j in range(4):
                    kt = 4 * n + j
                    i = dve.scalar_tensor_tensor(
                        out=yt_lo[:, ds(kt, 1), :], in0=tpk[:, j:j + 1, :],
                        scalar=vecs[:, ds(G_MEM + kt, 1)], in1=yt_hi[:, ds(kt, 1), :].bitcast(F32),
                        op0=ALU.mult, op1=ALU.subtract)
                i.then_inc(mem_lo, 1)

            def mixer_projection(n, m, first):
                for c in range(8):
                    split_lo(m, c)
                    if first and c == 2:
                        add_branches(NBLK - 1)
                    if first and c == 5:
                        merged_lo(NBLK - 1)
                    if not first and c == 1:
                        add_block(n - 1, m, 4)
                    if not first and c == 2:
                        memory_lo(n - 1)
                    if not first and c == 6:
                        block_lo(8 + n - 1, G_X, 4 * (n - 1))

            mixer_projection(0, m_wout, True)
            with dve.Fori(1, NBLK) as n:
                mixer_projection(n, m_wout + 2 * n, False)

            def attn_lo(hd):
                lo_of(mt_hi[:, ds(4 * hd, 4), :], mt_lo[:, ds(4 * hd, 4), :], xo_hi, hd + 1, xo_lo)

            def attn_head(hd, m, first):
                for c in range(24):
                    split_lo(m, c)
                    if first and c == 1:
                        add_block(NBLK - 1, m, 4)
                    if first and c == 2:
                        memory_lo(NBLK - 1)
                    if first and c == 4:
                        mean_square(sumsq_mem, meansq_mem, msm_ready, sqm_done, NBLK)
                    if first and c == 6:
                        block_lo(11, G_X, 12)
                    if first and c == 7:
                        mean_square(sumsq, meansq, ms_ready, sq_done, 12)
                    if not first and c == 4:
                        attn_lo(hd - 1)
                    if c == 21:
                        dve.wait_ge(sc_ps, hd + 1)
                        dve.tensor_reduce(smax[:, :], tpk[:, 0:2, :], AX_X, ALU.max)
                        dve.drain()
                        dve.tensor_scalar(nmax[:, :], smax[:, :], -XSCALE, None,
                                          ALU.mult).then_inc(nmax_ready, 1)
                    if c == 22:
                        dve.wait_ge(exp_ready, hd + 1)
                        dve.reciprocal(rinv[:, :], rowsum[:, :])
                        dve.drain()
                        for t in range(2):
                            i = dve.tensor_scalar(prob[:, t, :], prob[:, t, :], rinv[:, t:t + 1],
                                                  None, ALU.mult)
                        i.then_inc(prob_ready, 1)

            attn_head(0, m_xattn, True)
            with dve.Fori(1, HEADS) as hd:
                attn_head(hd, m_xattn + 6 * hd, False)

            def attn_projection(n, m, first):
                for c in range(8):
                    split_lo(m, c)
                    if first and c == 4:
                        attn_lo(HEADS - 1)
                    if not first and c == 1:
                        add_block(n - 1, m, 8)
                    if not first and c == 4:
                        block_lo(12 + n - 1, G_FFN2, 4 * (n - 1))

            attn_projection(0, m_wo, True)
            with dve.Fori(1, NBLK) as n:
                attn_projection(n, m_wo + 2 * n, False)
            add_half = ffn(1)
            apply_gain(2)
            for t in range(2):
                if t == 0:
                    dve.wait_ge(tile0_done, 2 * NBLK + 1)
                else:
                    dve.wait_ge(chunk_used, 4 * (m_ffn2 + 6 + 6 * LAST))
                hb = h[:, t, 3 * COLS:]
                dve.scalar_tensor_tensor(out=hb, in0=acc[:, t, :], scalar=0.5, in1=hb,
                                         op0=ALU.mult, op1=ALU.add).then_inc(h_added[1], 1)
            mean_square(sumsq, meansq, ms_ready, sq_done, 20)
            apply_gain(3)
            dve.wait_ge(rstd_ready, 5)
            for t, n in ((0, 0), (0, 1), (0, 2), (0, 3), (1, 3)):
                if n == 3:
                    dve.wait_ge(gfin_used, 4)
                hb = h[:, t, n * COLS:(n + 1) * COLS]
                dve.tensor_scalar(hb, hb, rstd[4][:, t:t + 1], None,
                                  ALU.mult).then_inc(scaled_v, 1)

        @block.tensor
        def _(pe):
            def chunk(m, c, hi, lo, kt, pair, first, last, tile_free=None,
                      tile0=None):
                pe.wait_ge(lo_done, 4 * m + c + 1)
                s = c % SLOTS
                for t in range(2):
                    if first and tile_free:
                        tile_free(t)
                    o = acc[:, pair + t, :]
                    for k in range(2):
                        a_hi, a_lo = hi[:, kt + k, tok(t)], lo[:, kt + k, tok(t)]
                        pe.matmul(o, a_hi, w_hi[:, s, k, :], start=first and k == 0, stop=False)
                        pe.matmul(o, a_hi, w_lo[:, s, k, :], start=False, stop=False)
                        i = pe.matmul(o, a_lo, w_hi[:, s, k, :], start=False, stop=last and k == 1)
                    if t == 0 and last and tile0:
                        i.then_inc(tile0, 1)
                i.then_inc(chunk_used, 1)

            def transpose_block(src, done):
                for j in range(4):
                    for t in range(2):
                        i = pe.transpose(tpk[:, j, tok(t)], src[:, t, j * P:(j + 1) * P], ident[:, :])
                i.then_inc(done, 1)

            def column_block(m, c0, hi, lo, pair, after=None, chunks=8, before=None,
                             tile_free=None, tile0=None):
                for c in range(chunks):
                    if before:
                        before(c0 + c)
                    chunk(m, c0 + c, hi, lo, 2 * c, pair, c == 0, c == chunks - 1,
                          tile_free, tile0)
                    if after:
                        after(c0 + c)

            def turn_h(n, b0):
                pe.wait_ge(hb_ready, 2 * (b0 - 8 + n) + 2)
                pe.wait_ge(blk_lo, b0 + n)
                transpose_block(nat, blk_ps)

            def ffn(f):
                m0 = ffn_parts[f][0]

                def down(m, c0, s, a_hi, a_lo, pairs, bank_free, after=None, tile0=None):
                    for c in range(8):
                        for at, taken, count in bank_free:
                            if c == at:
                                pe.wait_ge(taken, count)
                        chunk(m, c0 + c, a_hi, a_lo, 2 * (c % 2), pairs[c // 2],
                              c % 2 == 0, c % 2 == 1, tile0=tile0 if c == 7 else None)
                        if after:
                            after(c)

                def first_before(c):
                    if c < 8 and c % 2 == 0:
                        pe.wait_ge(blk_lo, (0 if f == 0 else 12) + c // 2 + 1)

                def first_after(c):
                    if f == 0 and c in (1, 3):
                        turn_input((c + 3) // 2)
                    if f == 0 and c == 9:
                        turn_parameters()
                    if f == 1 and c == 1:
                        turn_h(3, 12)

                column_block(m0, 0, xt_hi, xt_lo, 0, first_after, before=first_before)
                column_block(m0, 8, xt_hi, xt_lo, 2, first_after)

                def first_product(m, s):
                    def turn_hidden(c):
                        if c == 3:
                            pe.wait_ge(hid_ready[f], s)
                            transpose_block(hid, hid_ps[f])

                    pe.wait_ge(gate_ready[f], s)
                    column_block(m, 0, xt_hi, xt_lo, 0, turn_hidden)

                with pe.Fori(1, LAST) as s:
                    m = m0 + 4 + 6 * (s - 1)
                    first_product(m, s)
                    pe.wait_ge(ht_l[f], s)
                    down(m, 8, s - 1, ht_hi, ht_lo, (4, 2, 4, 0),
                         ((4, h_added[f], 4 * s - 3), (6, gate_ready[f], s + 1)))
                    pe.wait_ge(h_added[f], 4 * s - 2)
                    column_block(m, 16, xt_hi, xt_lo, 2)
                    pe.wait_ge(h_added[f], 4 * s)

                m = m0 + 4 + 6 * (LAST - 1)
                first_product(m, LAST)
                column_block(m, 8, xt_hi, xt_lo, 2)
                pe.wait_ge(ht_l[f], LAST)

                def turn_last(c):
                    if c == 3:
                        pe.wait_ge(hid_ready[f], SUPER)
                        transpose_block(hid, hid_ps[f])

                down(m, 16, LAST - 1, ht_hi, ht_lo, (4, 0, 4, 2),
                     ((2, gate_ready[f], SUPER), (4, h_added[f], 4 * LAST - 3),
                      (6, hid_ready[f], SUPER)), turn_last)
                pe.wait_ge(ht_l[f], SUPER)

                def last_after(c):
                    if f == 0 and c in (3, 6):
                        turn_residual((c - 3) // 3)

                down(m + 6, 0, LAST, yt_hi, yt_lo, (4, 2, 4, 0),
                     tuple((2 * n, h_added[f], 4 * LAST + (-1, 0, 1, -2)[n]) for n in range(4)),
                     last_after, tile0_done if f == 1 else None)

            def turn_residual(n):
                pe.wait_ge(h_added[0], 4 * LAST + n + 1)
                if n:
                    pe.wait_ge(blk_lo, 4 + n)
                transpose_block(h[:, :, n * COLS:(n + 1) * COLS], blk_ps)

            def turn_input(n):
                pe.wait_ge(x_in[n], 16)
                if n:
                    pe.wait_ge(blk_lo, n)
                transpose_block(h[:, :, n * COLS:(n + 1) * COLS], blk_ps)

            def turn_parameters():
                pe.wait_ge(vec_in, 80)
                pe.wait_ge(dt_rows, 1)
                pe.transpose(tp[:, 0, 0:VROWS], vrow[0:VROWS, :], ident[0:VROWS, 0:VROWS])
                pe.transpose(tp[:, 1, 0:96], prow[0:96, :], ident[0:96, 0:96]).then_inc(vecs_ps, 1)

            pe.wait_ge(ident_in, 16)
            pe.wait_ge(gain_in, 16)
            pe.transpose(acc[:, 4, 0:KT], vrow[0:KT, :], ident[0:KT, 0:KT]).then_inc(gain_ps, 1)
            turn_input(0)
            turn_input(1)
            ffn(0)

            def mix_ready(c):
                if c < 8 and c % 2 == 0:
                    pe.wait_ge(blk_lo, 4 + c // 2 + 1)

            def mix_after(c):
                if c in (1, 3):
                    turn_residual(2 + c // 2)
                if 4 <= c < 12:
                    g = c - 4
                    if g == 0:
                        pe.wait_ge(pads_ready, 1)
                        pe.wait_ge(h_added[0], 4 * LAST + 3)
                    if g >= 2:
                        pe.wait_ge(bc_ready, g - 1)
                    for j in range(4):
                        q = 4 * (g % 2) + j
                        if g < 4:
                            src = b_pad[:, (g // 2) % 2, 4 * q:4 * q + 4, :].rearrange("p a b -> p (a b)")
                        else:
                            src = c_pad[:, (g // 2) % 2, q, :]
                        i = pe.transpose(acc[:, 4 + g % 2, j * P:(j + 1) * P], src, ident[:, :])
                    i.then_inc(bc_ps, 1)
                if c == 11:
                    pe.wait_ge(u_nat, 1)
                    pe.wait_ge(blk_lo, 8)
                    transpose_block(nat, u_ps)

            column_block(m_mix, 0, xt_hi, xt_lo, 2, mix_after, before=mix_ready)
            pe.wait_ge(h_added[0], 4 * LAST + 4)
            column_block(m_mix, 8, xt_hi, xt_lo, 0, mix_after)

            def s5_products(hd, c, first):
                p = c // 3
                prev = p - 2
                if prev >= 0 or not first:
                    i4 = prev % 4
                    if prev in (0, 4):
                        pe.wait_ge(c_staged, 2 * hd + prev // 4 + 1)
                        if prev == 4 or not first:
                            pe.wait_ge(y_out, 2 * hd + prev // 4)
                    pe.wait_ge(s_ready, 8 * hd + p - 1)
                    o = acc[32 * i4:32 * i4 + 32, 5, 0:SEQ]
                    for part in range(2):
                        i = pe.matmul(o, c_st[:, part, 32 * i4:32 * i4 + 32],
                                      state[:, p % 2, part, :], start=part == 0, stop=part == 1)
                    i.then_inc(y_done, 1)
                if p < 8:
                    i4 = p % 4
                    if i4 == 0:
                        pe.wait_ge(b_staged, 2 * hd + p // 4 + 1)
                    if not (first and p == 0):
                        pe.wait_ge(x_free, 8 * hd + p)
                    for part in range(2):
                        i = pe.matmul(s5_in[:, part, :], b_st[32 * i4:32 * i4 + 32, part, :],
                                      u_st[32 * i4:32 * i4 + 32, :], start=True, stop=True)
                    i.then_inc(bu_done, 1)

            def retention_out(hd):
                pe.wait_ge(v_ready, 2 * hd + 2)
                pe.wait_ge(st_ready, hd + 1)
                pe.matmul(tp[:, 0, :], s_t[:, 0, tok(0)], v_r[:, 0, :], start=True, stop=True)
                pe.matmul(tp[:, 1, :], s_t[:, 0, tok(1)], v_r[:, 0, :], start=True, stop=False)
                pe.matmul(tp[:, 1, :], s_t[:, 1, tok(1)], v_r[:, 1, :], start=False,
                          stop=True).then_inc(pv_ps, 1)

            def head(hd, m, first):
                def after(c):
                    if c == 0 and not first:
                        retention_out(hd - 1)
                    if c % 3 == 0 and (first or c > 0):
                        s5_products(hd, c, first)
                    if first and c == 3:
                        pe.wait_ge(u_nat, 2)
                        pe.wait_ge(u_ready, 1)
                        transpose_block(nat, u_ps)
                    if not first and c == 6:
                        pe.wait_ge(on_ready, hd)
                        transpose_block(on, on_ps)
                    if c == 14:
                        pe.wait_ge(rot_ready, 2 * hd + 2)
                        if first:
                            pe.wait_ge(u_ready, 2)
                        else:
                            pe.wait_ge(on_lo, hd)
                        transpose_block(nat, qk_ps)
                    if c == 17:
                        pe.wait_ge(qk_ready, hd + 1)
                        for dt in range(2):
                            pe.matmul(tp[:, 0, 0:SEQ], qk_t[:, 2 + dt, tok(0)], qk_t[:, dt, :],
                                      start=dt == 0, stop=dt == 1)
                        for dt in range(2):
                            i = pe.matmul(tp[:, 0, 384:512], qk_t[:, 2 + dt, tok(1)],
                                          qk_t[:, dt, tok(1)], start=dt == 0, stop=dt == 1)
                        i.then_inc(st_ps, 1)

                def tile_free(t):
                    pe.wait_ge(v_ready, 2 * hd - 1 + t)

                if not first:
                    s5_products(hd, 0, False)
                column_block(m, 0, xt_hi, xt_lo, 2, after, tile_free=None if first else tile_free)
                if first:
                    pe.wait_ge(u_nat, 2)
                else:
                    pe.wait_ge(g_ready, hd)
                column_block(m, 8, xt_hi, xt_lo, 0, after)
                pe.wait_ge(qk_nat, hd + 1)
                column_block(m, 16, xt_hi, xt_lo, 2, after, tile0=v_tile0)

            head(0, m_heads, True)
            with pe.Fori(1, HEADS) as hd:
                head(hd, m_heads + 6 * hd, False)

            def merge(n, m, first):
                def before(c):
                    if first and c == 14:
                        pe.wait_ge(on_lo, HEADS)

                def after(c):
                    if first and c == 0:
                        retention_out(HEADS - 1)
                    if first and c in (0, 3):
                        pe.wait_ge(s_ready, 31 + c // 3)
                        i4 = 2 + c // 3
                        o = acc[32 * i4:32 * i4 + 32, 5, 0:SEQ]
                        for part in range(2):
                            i = pe.matmul(o, c_st[:, part, 32 * i4:32 * i4 + 32],
                                          state[:, c // 3, part, :], start=part == 0, stop=part == 1)
                        i.then_inc(y_done, 1)
                    if first and c == 6:
                        pe.wait_ge(on_ready, HEADS)
                        transpose_block(on, on_ps)
                    if not first and c == 3:
                        pe.wait_ge(mg_ready, n)
                        transpose_block(yb, mg_ps)

                pe.wait_ge(g_ready, HEADS) if first else pe.wait_ge(gb_ready, n)
                if first:
                    column_block(m, 0, xt_hi, xt_lo, 0, after)
                    pe.wait_ge(v_ready, 2 * HEADS)
                    column_block(m, 8, yt_hi, yt_lo, 2, before=before)
                else:
                    column_block(m, 0, yt_hi, yt_lo, 0, after)
                    pe.wait_ge(va_ready, n)
                    column_block(m, 8, xt_hi, xt_lo, 2)
                pe.wait_ge(ga_ready if first else yb_ready, n + 1)
                column_block(m, 16, xt_hi, xt_lo, 0)
                pe.wait_ge(yb_ready if first else ga_ready, n + 1)
                if first:
                    pe.wait_ge(gl_l, 1)
                column_block(m, 24, gl_hi, gl_lo, 2, chunks=4)
                pe.wait_ge(y_out, QT) if first else pe.wait_ge(sg_ready, n)
                column_block(m, 28, gl_hi, gl_lo, 4, chunks=4)

            merge(0, m_merge, True)
            with pe.Fori(1, NBLK) as n:
                merge(n, m_merge + 8 * n, False)

            def turn_memory(n):
                pe.wait_ge(mem_in, 16 * (n + 1))
                transpose_block(memb, mem_ps)

            def mixer_projection(n, m, first):
                def before(c):
                    if first and c == 6:
                        pe.wait_ge(mg_lo, NBLK)

                def after(c):
                    if first and c == 3:
                        pe.wait_ge(mg_ready, NBLK)
                        transpose_block(yb, mg_ps)
                    if not first and c == 3:
                        pe.wait_ge(mem_lo, n)
                        turn_h(n - 1, 8)
                    if c == 7:
                        if not first:
                            pe.wait_ge(blk_lo, 8 + n)
                        turn_memory(n)

                def tile_free(t):
                    pe.wait_ge(hb_ready, 2 * n - 1 + t)

                if first:
                    pe.wait_ge(va_ready, NBLK)
                column_block(m, 0, mt_hi, mt_lo, 2, after, before=before,
                             tile_free=None if first else tile_free, tile0=tile0_done)

            mixer_projection(0, m_wout, True)
            with pe.Fori(1, NBLK) as n:
                mixer_projection(n, m_wout + 2 * n, False)

            def attn_pv(hd):
                pe.wait_ge(vx_ready, hd + 1)
                pe.wait_ge(pt_ready, hd + 1)
                for d in range(4):
                    for mt in range(2):
                        i = pe.matmul(tpk[:, d, :], v_x[:, mt, d * P:(d + 1) * P], prob_t[:, mt, :],
                                      start=mt == 0, stop=mt == 1)
                i.then_inc(xo_ps, 1)

            def attn_head(hd, m, first):
                def after(c):
                    if c == 1 and not first:
                        attn_pv(hd - 1)
                    if c == 3 and first:
                        pe.wait_ge(mem_lo, NBLK)
                        turn_h(3, 8)
                    if c == 10:
                        pe.wait_ge(kn_ready, hd + 1)
                        pe.wait_ge(blk_lo, 12) if first else pe.wait_ge(xo_lo, hd)
                        transpose_block(nat, kx_ps)
                    if c == 17:
                        pe.wait_ge(qn_ready, hd + 1)
                        pe.wait_ge(kx_ready, hd + 1)
                        transpose_block(nat, qx_ps)
                    if c == 19:
                        pe.wait_ge(qx_ready, hd + 1)
                        for t in range(2):
                            for d in range(4):
                                i = pe.matmul(tpk[:, t, :], q_x[:, d, tok(t)], k_x[:, d, :],
                                              start=d == 0, stop=d == 3)
                        i.then_inc(sc_ps, 1)
                    if c == 21:
                        pe.wait_ge(prob_ready, hd + 1)
                        for mt in range(2):
                            for t in range(2):
                                i = pe.transpose(tpk[:, 2 + mt, tok(t)], prob[:, t, tok(mt)],
                                                 ident[:, :])
                        i.then_inc(pt_ps, 1)

                def before(c):
                    if first and c == 6:
                        pe.wait_ge(mem_lo, NBLK)

                if not first:
                    pe.wait_ge(kn_ready, hd)
                column_block(m, 0, yt_hi, yt_lo, 0, after, before=before)
                if first:
                    pe.wait_ge(blk_lo, 12)
                else:
                    pe.wait_ge(qn_ready, hd)
                column_block(m, 8, xt_hi, xt_lo, 2, after)
                if first:
                    pe.wait_ge(sg_ready, NBLK)
                else:
                    pe.wait_ge(vx_ready, hd)
                column_block(m, 16, yt_hi, yt_lo, 4, after)

            attn_head(0, m_xattn, True)
            with pe.Fori(1, HEADS) as hd:
                attn_head(hd, m_xattn + 6 * hd, False)

            def attn_projection(n, m, first):
                def before(c):
                    if first and c == 6:
                        pe.wait_ge(xo_lo, HEADS)

                def after(c):
                    if c == 1:
                        if first:
                            attn_pv(HEADS - 1)
                        else:
                            turn_h(n - 1, 12)

                def tile_free(t):
                    pe.wait_ge(hb_ready, 2 * (4 + n) - 1 + t)

                if first:
                    pe.wait_ge(qn_ready, HEADS)
                column_block(m, 0, mt_hi, mt_lo, 2, after, before=before,
                             tile_free=None if first else tile_free, tile0=tile0_done)

            attn_projection(0, m_wo, True)
            with pe.Fori(1, NBLK) as n:
                attn_projection(n, m_wo + 2 * n, False)
            ffn(1)

        @block.gpsimd
        def _(pool):
            def tt(o, a, b, op):
                return pool.tensor_tensor(o, a, b, op)

            def norm_factor(dst, src, ready, count, done):
                pool.wait_ge(ready, count)
                tt(dst[:, :], src[:, :], mhalf[:, :], ALU.pow).then_inc(done, 1)

            for row, v in ((G_MIX, mix_norm), (G_X, xattn_norm),
                           (G_MEM, mem_norm), (G_FFN2, ffn2_norm), (G_D, s5_d)):
                k = v.shape[1] // P
                pool.dma_start(vrow[row:row + k, :],
                               v.rearrange("o (k p) -> (o k) p", p=P)).then_inc(vec_in, 16)
            pool.dma_start(prow[0:32, :], s5_a_re.rearrange("o (j g) p -> (o j) (g p)", g=2)
                           ).then_inc(par_in, 16)
            pool.dma_start(prow[32:64, :], s5_a_im.rearrange("o (j g) p -> (o j) (g p)", g=2)
                           ).then_inc(par_in, 16)
            pool.dma_start(dt_row[64:96, :], s5_log_dt.rearrange("o (j g) -> (o j) g", g=2)
                           ).then_inc(par_in, 16)
            pool.dma_start(parity[:, :], c_parity).then_inc(bc_in, 16)
            for part, (b, c) in enumerate(((s5_b_re, s5_c_re), (s5_b_im, s5_c_im))):
                for g in range(2):
                    pool.dma_start(b_raw[64 * g:64 * g + 64, part, :, :],
                                   b[0].rearrange("(j g) p c -> g p j c", g=2)[g]
                                   ).then_inc(bc_in, 16)
                pool.dma_start(c_raw[:, part, :, :],
                               c[0].rearrange("(q g) c p -> (g c) q p", g=8)).then_inc(bc_in, 16)
            norm_factor(rstd[0], meansq, ms_ready, 1, rstd_ready)

            v = lambda i: par[:, i, :]
            pool.wait_ge(exp_dt, 1)
            tt(v(4), v(0), v(3), ALU.mult)
            tt(v(5), v(1), v(3), ALU.mult)
            pool.drain()
            pool.tensor_scalar(v(6), v(5), 1.0 / (2 * math.pi), ROUND, ALU.mult, ALU.add)
            pool.drain()
            pool.tensor_scalar(v(6), v(6), -ROUND, None, ALU.add)
            pool.drain()
            for k, part in enumerate((TWO_PI_A, TWO_PI_B, TWO_PI_C)):
                pool.tensor_scalar(v(8), v(6), part, None, ALU.mult)
                pool.drain()
                tt(v(7), v(5 if k == 0 else 7), v(8), ALU.subtract)
                pool.drain()
            pool.tensor_scalar(v(7), v(7), math.pi - 1e-6, -(math.pi - 1e-6), ALU.min,
                               ALU.max).then_inc(angles, 1)
            pool.wait_ge(trig, 1)
            tt(v(11), v(9), v(9), ALU.mult)
            pool.drain()
            pool.tensor_scalar(v(12), v(11), -2.0, 1.0, ALU.mult, ALU.add)
            pool.drain()
            tt(v(13), mag[:, :], v(12), ALU.mult)
            tt(v(14), mag[:, :], v(10), ALU.mult)
            tt(v(15), v(0), v(0), ALU.mult)
            tt(v(16), v(1), v(1), ALU.mult)
            pool.drain()
            pool.tensor_scalar(v(13), v(13), -1.0, None, ALU.add)
            tt(v(15), v(15), v(16), ALU.add)
            pool.memset(v(25), -1.0)
            pool.drain()
            tt(v(16), v(15), v(25), ALU.pow)
            for o, a, b in ((17, 13, 0), (18, 14, 1), (19, 14, 0), (20, 13, 1)):
                tt(v(o), v(a), v(b), ALU.mult)
            pool.drain()
            tt(v(21), v(17), v(18), ALU.add)
            tt(v(22), v(19), v(20), ALU.subtract)
            pool.drain()
            tt(v(23), v(21), v(16), ALU.mult)
            tt(v(24), v(22), v(16), ALU.mult)
            pool.drain()

            def complex_product(o_re, o_im, a_re, a_im, b_re, b_im, width):
                t1 = pow_tmp[:, 0, :, 0:width]
                t2 = pow_tmp[:, 1, :, 0:width]
                tt(t1, a_re, b_re, ALU.mult)
                tt(t2, a_im, b_im, ALU.mult)
                pool.drain()
                tt(o_re, t1, t2, ALU.subtract)
                pool.drain()
                tt(t1, a_re, b_im, ALU.mult)
                tt(t2, a_im, b_re, ALU.mult)
                pool.drain()
                tt(o_im, t1, t2, ALU.add)
                pool.drain()

            e_re, e_im = v(12).unsqueeze(2), v(10).unsqueeze(2)
            n_re, n_im = v(5).unsqueeze(2), v(6).unsqueeze(2)
            for re, im in ((2, 3), (0, 1)):
                pool.memset(s5_tab[:, re, :, 0:1], 1.0)
                pool.memset(s5_tab[:, im, :, 0:1], 0.0)
                pool.drain()
                width = 1
                while width < HALF:
                    complex_product(s5_tab[:, re, :, width:2 * width], s5_tab[:, im, :, width:2 * width],
                                    s5_tab[:, re, :, 0:width], s5_tab[:, im, :, 0:width],
                                    e_re.broadcast_to([P, PAIRS, width]),
                                    e_im.broadcast_to([P, PAIRS, width]), width)
                    complex_product(n_re, n_im, e_re, e_im, e_re, e_im, 1)
                    e_re, e_im, n_re, n_im = n_re, n_im, e_re, e_im
                    width *= 2

            pool.wait_ge(bc_in, 16 * 7)
            pool.memset(b_pad[:, :, :, :], 0.0)
            f_re = v(23).unsqueeze(2).broadcast_to([P, PAIRS, HALF])
            f_im = v(24).unsqueeze(2).broadcast_to([P, PAIRS, HALF])
            for part in range(2):
                tt(pow_tmp[:, 0, :, :], f_re, b_raw[:, part, :, :], ALU.mult)
                tt(pow_tmp[:, 1, :, :], f_im, b_raw[:, 1 - part, :, :], ALU.mult)
                pool.drain()
                for g in range(2):
                    half = slice(64 * g, 64 * g + 64)
                    tt(b_pad[half, part, :, HALF * g:HALF * (g + 1)], pow_tmp[half, 0, :, :],
                       pow_tmp[half, 1, :, :], ALU.add if part else ALU.subtract)
                pool.drain()
            for part, sign in ((0, 1.0), (1, -1.0)):
                for g in range(2):
                    i = pool.tensor_scalar(c_pad[:, part, :, 64 * g:64 * g + 64],
                                           c_raw[:, part, :, :], parity[:, g:g + 1], sign,
                                           ALU.mult, ALU.mult)
            i.then_inc(pads_ready, 1)

            norm_factor(rstd[1], meansq, ms_ready, 2, rstd_ready)
            pool.wait_ge(bc_ready, 8)

            def table(pair, buf):
                hi_re = s5_tab[:, 0, ds(pair, 1), :].rearrange("p o (a b) -> p o a b", b=1)
                hi_im = s5_tab[:, 1, ds(pair, 1), :].rearrange("p o (a b) -> p o a b", b=1)
                low = s5_tab[:, 2:4, ds(pair, 1), :].broadcast_to([P, 2, HALF, HALF])
                cs = tab[:, buf, :, :].rearrange("p r (a b) -> p r a b", b=HALF)
                tmp = pool_tmp[:, :, :].rearrange("p r (a b) -> p r a b", b=HALF)
                tt(cs, hi_re.broadcast_to([P, 2, HALF, HALF]), low, ALU.mult)
                tt(tmp, hi_im.broadcast_to([P, 2, HALF, HALF]), low, ALU.mult)
                pool.drain()
                tt(tab[:, buf, 0, :], tab[:, buf, 0, :], pool_tmp[:, 1, :], ALU.subtract)
                tt(tab[:, buf, 1, :], tab[:, buf, 1, :], pool_tmp[:, 0, :],
                   ALU.add).then_inc(tab_ready, 1)
                pool.drain()

            def turn_back(hd, p, first):
                buf = p % 2
                pool.wait_ge(z_ready, 8 * hd + p + 1)
                if not (first and p < 2):
                    pool.wait_ge(y_done, 8 * hd + p - 1)
                z = zb[:, buf, :, :]
                tt(state[:, buf, :, :], z, tab[:, buf, 0:1, :].broadcast_to([P, 2, SEQ]), ALU.mult)
                tt(pool_tmp[:, :, :], z, tab[:, buf, 1:2, :].broadcast_to([P, 2, SEQ]), ALU.mult)
                pool.drain()
                tt(state[:, buf, 0, :], state[:, buf, 0, :], pool_tmp[:, 1, :], ALU.subtract)
                tt(state[:, buf, 1, :], state[:, buf, 1, :], pool_tmp[:, 0, :],
                   ALU.add).then_inc(s_ready, 1)
                pool.drain()

            def head(hd, first, last):
                for p in range(8):
                    if not (last and p == 7):
                        table(8 * hd + p + 1, (p + 1) % 2)
                    turn_back(hd, p, first)
                    if p == 0 and not first:
                        norm_factor(grstd, vare, var_ready, hd, grstd_ready)

            table(0, 0)
            head(0, True, False)
            with pool.Fori(1, HEADS - 1) as hd:
                head(hd, False, False)
            head(HEADS - 1, False, True)
            norm_factor(grstd, vare, var_ready, HEADS, grstd_ready)

            pool.wait_ge(mg_ready, 1)

            def load_mem(n):
                pool.dma_start(memb[:, :, :], mem[0][:, ds(n * COLS, COLS)].rearrange(
                    "(t p) d -> p t d", p=P)).then_inc(mem_in, 16)

            load_mem(0)
            with pool.Fori(1, NBLK) as n:
                pool.wait_ge(mem_ps, n)
                pool.wait_ge(sqm_done, n)
                load_mem(n)
            norm_factor(rstd_mem, meansq_mem, msm_ready, 1, rstdm_ready)
            norm_factor(rstd[2], meansq, ms_ready, 3, rstd_ready)
            norm_factor(rstd[3], meansq, ms_ready, 4, rstd_ready)
            pool.wait_ge(hid_ready[1], 1)
            pool.dma_start(gfin[:, :], final_norm.rearrange("(o d) -> o d", o=1).broadcast_to([P, D])
                           ).then_inc(gfin_in, 16)
            norm_factor(rstd[4], meansq, ms_ready, 5, rstd_ready)


_INS = ['x', 'mem', 'ffn1_norm', 'ffn1_w1', 'ffn1_w3', 'ffn1_w2', 'mix_norm', 'w_in', 's5_a_re',
        's5_a_im', 's5_log_dt', 's5_b_re', 's5_b_im', 's5_c_re', 's5_c_im', 's5_d', 's5_glu_v',
        's5_glu_g', 'ret_w_o', 'w_out', 'xattn_norm', 'mem_norm', 'xattn_wq', 'xattn_wk',
        'xattn_wv', 'xattn_wo', 'ffn2_norm', 'ffn2_w1', 'ffn2_w3', 'ffn2_w2', 'final_norm']
_OUTS = [((1, 256, 2048), 'float32')]


def _constants():
    import numpy as np
    inv = 10000.0 ** (-np.arange(0, 256, 2, dtype=np.float32) / np.float32(256))
    ang = np.arange(256, dtype=np.float32)[:, None] * inv.astype(np.float32)[None, :]
    ang = ang.astype(np.float32).astype(np.float64)
    rope = np.stack([np.cos(ang), np.sin(ang)], 1).reshape(2, 128, 2, 128).transpose(1, 0, 2, 3)
    i = np.arange(256)
    rel = (i[None, :] - i[:, None]).astype(np.float64)
    decay = np.zeros((4, 128, 384))
    for hd in range(4):
        full = np.where(rel >= 0, (1.0 - 2.0 ** (-5.0 - hd)) ** np.maximum(rel, 0), 0.0) / 16.0
        decay[hd, :, 0:256] = full[0:128]
        decay[hd, :, 256:384] = full[128:256, 128:256]
    group = np.arange(128) // 16
    parity = np.stack([group % 2 == 0, group % 2 == 1], 1)
    return {
        "ident": np.eye(128, dtype=np.float32),
        "rope": np.ascontiguousarray(rope, dtype=np.float32),
        "decay": decay.reshape(512, 384).astype(np.float32),
        "parity": parity.astype(np.float32),
    }


def kernel(**inputs):
    import numpy as _np
    import concourse.bacc as _bacc
    from concourse import mybir as _mybir
    from concourse.bass_utils import run_bass_kernel_spmd as _run

    nc = _bacc.Bacc("TRN2", target_bir_lowering=False, num_devices=1)
    arrays, args = {}, []
    for name in _INS:
        a = _np.ascontiguousarray(inputs[name])
        arrays[f"in_{name}_dram"] = a
        args.append(nc.dram_tensor(f"in_{name}_dram", a.shape, _mybir.dt.from_np(a.dtype), kind="ExternalInput").ap())
    for name, a in _constants().items():
        arrays[f"c_{name}_dram"] = a
        args.append(nc.dram_tensor(f"c_{name}_dram", a.shape, _mybir.dt.from_np(a.dtype), kind="ExternalInput").ap())
    for i, (shape, dtype) in enumerate(_OUTS):
        dt = _mybir.dt.from_np(_np.dtype(dtype))
        args.append(nc.dram_tensor(f"out_{i}_dram", shape, dt, kind="ExternalOutput").ap())
    build(nc, *args)
    r = _run(nc, [arrays], core_ids=[0])
    return r.results[0]["out_0_dram"]
```

```python
import math
from contextlib import ExitStack

import concourse.bass as bass
from concourse import mybir

F32 = mybir.dt.float32
F32R = mybir.dt.float32r
ACT = mybir.ActivationFunctionType
ALU = mybir.AluOpType
AX_X = mybir.AxisListType.X

P = 128
SLOTS = 4
COLS = 512
D = 2048
SEQ = 256
KT = D // P
SUPER = 5632 // COLS
LAST = SUPER - 1
HEADS = 4
NBLK = D // COLS
QT = 1024 // P
PAIRS = 32
DOUBLES = 2 * HEADS
HALF = 16
RMS_EPS = 1e-6
GN_EPS = 1e-5
XSCALE = 512 ** -0.5
C_Q, C_V, C_G, C_GA, C_GB = 1024, 3072, 5120, 7168, 9216
G_FFN1, G_MIX, G_X, G_MEM, G_FFN2, G_D, VROWS = 0, 16, 32, 48, 64, 80, 88
ROUND = 1.5 * 2.0 ** 23
TWO_PI_A = 6.28125
TWO_PI_B = 4058 / 2.0 ** 21
TWO_PI_C = 2 * math.pi - TWO_PI_A - TWO_PI_B


def ds(start, size):
    return bass.ds(start, size)


def tok(t):
    return slice(t * P, (t + 1) * P)


def build(nc, x, mem, ffn1_norm, ffn1_w1, ffn1_w3, ffn1_w2, mix_norm, w_in, s5_a_re, s5_a_im,
          s5_log_dt, s5_b_re, s5_b_im, s5_c_re, s5_c_im, s5_d, s5_glu_v, s5_glu_g, ret_w_o, w_out,
          xattn_norm, mem_norm, xattn_wq, xattn_wk, xattn_wv, xattn_wo, ffn2_norm, ffn2_w1, ffn2_w3,
          ffn2_w2, final_norm, c_ident, c_rope, c_decay, c_parity, out):
    m_ffn1 = 0
    m_mix = m_ffn1 + 4 + 6 * LAST + 2
    m_heads = m_mix + 4
    m_merge = m_heads + 6 * HEADS
    m_wout = m_merge + 8 * NBLK
    m_xattn = m_wout + 2 * NBLK
    m_wo = m_xattn + 6 * HEADS
    m_ffn2 = m_wo + 2 * NBLK

    with ExitStack() as ctx:
        def sb(name, shape, dt=F32, where=ctx):
            return where.enter_context(nc.sbuf_tensor(name, shape, dt))

        def sem(name):
            return ctx.enter_context(nc.semaphore(name))

        h = sb("h", [P, 2, D])
        xt_hi = sb("xt_hi", [P, KT, SEQ], F32R)
        xt_lo = sb("xt_lo", [P, KT, SEQ], F32R)
        yt_hi = sb("yt_hi", [P, KT, SEQ], F32R)
        yt_lo = sb("yt_lo", [P, KT, SEQ], F32R)
        raw = sb("raw", [P, SLOTS, 2, COLS])
        w_hi = sb("w_hi", [P, SLOTS, 2, COLS], F32R)
        w_lo = sb("w_lo", [P, SLOTS, 2, COLS], F32R)
        nat = sb("nat", [P, 2, COLS])
        ident = sb("ident", [P, P])
        vecs = sb("vecs", [P, VROWS])
        sumsq = sb("sumsq", [P, 2, NBLK])
        meansq = sb("meansq", [P, 2])
        sumsq_mem = sb("sumsq_mem", [P, 2, NBLK])
        meansq_mem = sb("meansq_mem", [P, 2])
        mhalf = sb("mhalf", [P, 2])
        rstd = [sb(f"rstd{i}", [P, 2]) for i in range(5)]
        rstd_mem = sb("rstd_mem", [P, 2])
        mag = sb("mag", [P, PAIRS])

        with ExitStack() as plan:
            s5_tab = sb("s5_tab", [P, 4, PAIRS, HALF], F32, plan)
            b_t = sb("b_t", [P, 2, QT, P], F32, plan)
            c_t = sb("c_t", [P, 2, QT, P], F32, plan)
            u_t = sb("u_t", [P, QT, SEQ], F32, plan)
            with ExitStack() as part:
                gate = sb("gate", [P, 2, COLS], F32, part)
                hid = sb("hid", [P, 2, COLS], F32, part)
                ht_hi = sb("ht_hi", [P, 4, SEQ], F32R, part)
                ht_lo = sb("ht_lo", [P, 4, SEQ], F32R, part)
                junk = sb("junk", [P, COLS], F32, part)
                par = sb("par", [P, 26, PAIRS], F32, part)
                vrow = sb("vrow", [P, P], F32, part)
                prow = sb("prow", [P, P], F32, part)
                dt_row = sb("dt_row", [P, 2], F32, part)
                parity = sb("parity", [P, 2], F32, part)
                b_pad = sb("b_pad", [P, 2, PAIRS, 32], F32, part)
                c_pad = sb("c_pad", [P, 2, QT, P], F32, part)
            with ExitStack() as part:
                bu_parts = sb("bu_parts", [P, 4, SEQ], F32R, part)
                c_st = sb("c_st", [P, 2, P], F32, part)
                zb = sb("zb", [P, 2, 2, SEQ], F32, part)
                rot2 = sb("rot2", [P, 2, SEQ], F32, part)
                tab = sb("tab", [P, 2, 2, SEQ], F32, part)
                state = sb("state", [P, 2, 2, SEQ], F32, part)
                pool_tmp = sb("pool_tmp", [P, 2, SEQ], F32, part)
                on = sb("on", [P, 2, COLS], F32, part)
                qk_t = sb("qk_t", [P, 4, SEQ], F32, part)
                v_r = sb("v_r", [P, 2, COLS], F32, part)
                g_r = sb("g_r", [P, 2, COLS], F32, part)
                s_t0 = sb("s_t0", [P, SEQ], F32, part)
                s_t1 = sb("s_t1", [P, P], F32, part)
                rope = sb("rope", [P, 2, 2, P], F32, part)
                decay = sb("decay", [P, 384], F32, part)
                bstat = sb("bstat", [P, 2, 6], F32, part)
                mv = sb("mv", [P, 2, 2], F32, part)
                vare = sb("vare", [P, 2], F32, part)
                grstd = sb("grstd", [P, 2], F32, part)
        with ExitStack() as plan:
            sb("under_b_t", [P, 4, PAIRS, HALF], F32, plan)
            pow_tmp = sb("pow_tmp", [P, 2, PAIRS, HALF], F32, plan)
            sb("rest_of_b_t", [P, 2, PAIRS, HALF], F32, plan)
            b_raw = sb("b_raw", [P, 2, PAIRS, HALF], F32, plan)
            c_raw = sb("c_raw", [P, 2, QT, 64], F32, plan)
        with ExitStack() as plan:
            mt_hi = sb("mt_hi", [P, KT, SEQ], F32R, plan)
            mt_lo = sb("mt_lo", [P, KT, SEQ], F32R, plan)
            with ExitStack() as part:
                yb = sb("yb", [P, 2, COLS], F32, part)
                ga = sb("ga", [P, 2, COLS], F32, part)
                gb = sb("gb", [P, 2, COLS], F32, part)
                sg = sb("sg", [P, 2, COLS], F32, part)
                gl_hi = sb("gl_hi", [P, QT, SEQ], F32R, part)
                gl_lo = sb("gl_lo", [P, QT, SEQ], F32R, part)
                memb = sb("memb", [P, 2, COLS], F32, part)
                junk2 = sb("junk2", [P, COLS], F32, part)
            with ExitStack() as part:
                kx_hi = sb("kx_hi", [P, 4, SEQ], F32R, part)
                kx_lo = sb("kx_lo", [P, 4, SEQ], F32R, part)
                qx_hi = sb("qx_hi", [P, 4, SEQ], F32R, part)
                qx_lo = sb("qx_lo", [P, 4, SEQ], F32R, part)
                vx_hi = sb("vx_hi", [P, 2, COLS], F32R, part)
                vx_lo = sb("vx_lo", [P, 2, COLS], F32R, part)
                prob = sb("prob", [P, 2, SEQ], F32, part)
                pt_hi = sb("pt_hi", [P, 2, SEQ], F32R, part)
                pt_lo = sb("pt_lo", [P, 2, SEQ], F32R, part)
                smax = sb("smax", [P, 2], F32, part)
                nmax = sb("nmax", [P, 2], F32, part)
                rowsum = sb("rowsum", [P, 2], F32, part)
                rinv = sb("rinv", [P, 2], F32, part)
        with ExitStack() as plan:
            gfin = sb("gfin", [P, D], F32, plan)
        bu_stack = [yt_hi[0:96, kt:kt + 2, :] for kt in (KT - 4, KT - 2)]

        acc = ctx.enter_context(nc.psum_tensor("acc", [P, 6, COLS], F32))
        tp = ctx.enter_context(nc.psum_tensor("tp", [P, 2, COLS], F32))
        tpk = tp[:, :, :].rearrange("p b (j s) -> p (b j) s", s=SEQ)
        input_banks = (tpk, *(acc[:, b:b + 2, :].rearrange("p b (j s) -> p (b j) s", s=SEQ)
                              for b in (2, 4)), tpk)
        s5_in = acc[:, 4, :].rearrange("p (r s) -> p r s", r=2)
        s5_out = acc[:, 5, 0:SEQ]

        raw_in = [sem(f"raw_in{i}") for i in range(SLOTS)]
        hi_done, lo_done, chunk_used = sem("hi_done"), sem("lo_done"), sem("chunk_used")
        tile0_done, v_tile0 = sem("tile0_done"), sem("v_tile0")
        ident_in, vec_in, par_in, bc_in, rope_in, decay_in, mem_in, gfin_in = (sem(n) for n in (
            "ident_in", "vec_in", "par_in", "bc_in", "rope_in", "decay_in", "mem_in", "gfin_in"))
        x_in = [sem(f"x_in{n}") for n in range(NBLK)]
        gain_in, gain_ps, gain_ready = sem("gain_in"), sem("gain_ps"), sem("gain_ready")
        x0_in, x0_ps, x0_hi, x0_lo = sem("x0_in"), sem("x0_ps"), sem("x0_hi"), sem("x0_lo")
        dt_rows, vecs_ps, par_ready, exp_dt, angles, trig = (
            sem(n) for n in ("dt_rows", "vecs_ps", "par_ready", "exp_dt", "angles",
                             "trig"))
        pads_ready, bc_ps, bc_ready = sem("pads_ready"), sem("bc_ps"), sem("bc_ready")
        blk_ps, blk_hi, blk_lo, sq_done, hb_ready = (sem(n) for n in (
            "blk_ps", "blk_hi", "blk_lo", "sq_done", "hb_ready"))
        ms_ready, rstd_ready = sem("ms_ready"), sem("rstd_ready")
        gate_ready, hid_ready, hid_ps, ht_h, ht_l, h_added = (
            [sem(f"{n}{f}") for f in range(2)]
            for n in ("gate_ready", "hid_ready", "hid_ps", "ht_h", "ht_l", "h_added"))
        stack_in = [sem(f"stack_in{i}") for i in range(2)]
        u_nat, u_ps, u_ready, b_staged, b_split, c_staged, bu_done, x_free, tab_ready, z_ready, \
            s_ready, y_done, y_out, gelu_done, gl_h, gl_l = (sem(n) for n in (
                "u_nat", "u_ps", "u_ready", "b_staged", "b_split", "c_staged", "bu_done", "x_free",
                "tab_ready", "z_ready", "s_ready", "y_done", "y_out", "gelu_done", "gl_h", "gl_l"))
        qk_nat, rot_ready, qk_ps, qk_ready, st_ps, st_ready, g_ready, v_ready, pv_ps, var_ready, \
            grstd_ready, og_ready, on_ready, on_ps, on_hi, on_lo = (sem(n) for n in (
                "qk_nat", "rot_ready", "qk_ps", "qk_ready", "st_ps", "st_ready", "g_ready",
                "v_ready", "pv_ps", "var_ready", "grstd_ready", "og_ready", "on_ready", "on_ps",
                "on_hi", "on_lo"))
        yb_ready, ga_ready, gb_ready, sg_ready, va_ready, mg_ready, mg_ps, mg_hi, mg_lo = (
            sem(n) for n in ("yb_ready", "ga_ready", "gb_ready", "sg_ready", "va_ready",
                             "mg_ready", "mg_ps", "mg_hi", "mg_lo"))
        mem_ps, mem_hi, mem_lo, sqm_done, msm_ready, rstdm_ready = (sem(n) for n in (
            "mem_ps", "mem_hi", "mem_lo", "sqm_done", "msm_ready", "rstdm_ready"))
        kn_ready, kx_ps, kx_h, kx_l, qn_ready, qx_ps, qx_h, qx_l, sc_ps, nmax_ready, exp_ready, \
            prob_ready, pt_ps, pt_h, pt_l, vx_h, vx_l, xo_ps, xo_hi, xo_lo = (sem(n) for n in (
                "kn_ready", "kx_ps", "kx_h", "kx_l", "qn_ready", "qx_ps", "qx_h", "qx_l", "sc_ps",
                "nmax_ready", "exp_ready", "prob_ready", "pt_ps", "pt_h", "pt_l", "vx_h", "vx_l",
                "xo_ps", "xo_hi", "xo_lo"))
        gfin_used, scaled_v, scaled_s, out_done = (
            sem(n) for n in ("gfin_used", "scaled_v", "scaled_s", "out_done"))

        ffn_parts = (
            (m_ffn1, ffn1_w1[0], ffn1_w3[0], ffn1_w2[0], 0),
            (m_ffn2, ffn2_w1[0], ffn2_w3[0], ffn2_w2[0], 3),
        )

        block = ctx.enter_context(nc.Block())

        @block.sync
        def _(sp):
            def fetch(m, c, src):
                if not (isinstance(m, int) and 4 * m + c < SLOTS):
                    sp.wait_ge(lo_done, 4 * m + c - SLOTS + 1)
                sp.dma_start(raw[:, c % SLOTS, :, :], src).then_inc(raw_in[c % SLOTS], 16)

            def piece(w, row, col):
                return w[ds(row, 2 * P), ds(col, COLS)].rearrange("(k p) n -> p k n", p=P)

            def column_block(m, c0, w, col, chunks=8):
                for c in range(chunks):
                    fetch(m, c0 + c, piece(w, 2 * P * c, col))

            def ffn(f):
                m0, w1, w3, w2, _ = ffn_parts[f]

                def down(m, c0, s):
                    for c in range(8):
                        fetch(m, c0 + c, piece(w2, s * COLS + 2 * P * (c % 2), COLS * (c // 2)))

                for c in range(8):
                    fetch(m0, c, piece(w1, 2 * P * c, 0))
                    if f == 0 and c in (0, 1, 3, 5):
                        n = (c + 1) // 2
                        load_x(x_in[n], n * COLS if n else 2 * P, (n + 1) * COLS)
                column_block(m0, 8, w3, 0)
                with sp.Fori(1, LAST) as s:
                    m = m0 + 4 + 6 * (s - 1)
                    column_block(m, 0, w1, s * COLS)
                    down(m, 8, s - 1)
                    column_block(m, 16, w3, s * COLS)
                m = m0 + 4 + 6 * (LAST - 1)
                column_block(m, 0, w1, LAST * COLS)
                column_block(m, 8, w3, LAST * COLS)
                down(m, 16, LAST - 1)
                down(m + 6, 0, LAST)

            def load_x(done, start, end):
                sp.dma_start(h[:, :, start:end],
                             x[0, :, start:end].rearrange("(t p) d -> p t d", p=P)
                             ).then_inc(done, 16)

            sp.dma_start(ident[:, :], c_ident).then_inc(ident_in, 16)
            sp.dma_start(vrow[0:KT, :], ffn1_norm.rearrange("o (k p) -> (o k) p", p=P)
                         ).then_inc(gain_in, 16)
            load_x(x0_in, 0, 2 * P)
            ffn(0)

            w = w_in[0]
            column_block(m_mix, 0, w, 0)
            column_block(m_mix, 8, w, COLS)

            def load_stack(hd, p, first):
                if p in (0, 4):
                    sp.wait_ge(b_split, 2 * hd + p // 4 + 1)
                elif not (first and p < 2):
                    sp.wait_ge(bu_done, 8 * hd + p - 1)
                rows = slice(32 * (p % 4), 32 * (p % 4) + 32)
                for row, parts in ((0, slice(0, 3, 2)), (32, slice(0, 4, 3)), (64, slice(1, 3))):
                    sp.dma_start(bu_stack[p % 2][row:row + 32, :, :].bitcast(F32),
                                 bu_parts[rows, parts, :].bitcast(F32)
                                 ).then_inc(stack_in[p % 2], 16)

            def head_chunks(hd, m, first):
                for c in range(24):
                    if c == 2 and not first:
                        load_stack(hd - 1, 7, False)
                    if c > 3 and c % 3 == 2:
                        load_stack(hd, (c - 5) // 3, first)
                    if c < 8:
                        sp.wait_ge(lo_done, 4 * m + c - SLOTS + 1)
                        for b in range(2):
                            sp.dma_start(
                                raw[:, c % SLOTS, :, b * SEQ:(b + 1) * SEQ],
                                w[2 * P * c:2 * P * (c + 1), ds(C_Q + 1024 * b + hd * SEQ, SEQ)]
                                .rearrange("(k p) n -> p k n", p=P)).then_inc(raw_in[c % SLOTS], 16)
                    else:
                        col = (C_G if c < 16 else C_V) + hd * COLS
                        fetch(m, c, piece(w, 2 * P * (c % 8), col))
                    if c == 4:
                        if first:
                            sp.wait_ge(bc_ps, 8)
                            sp.dma_start(rope[:, :, :, :], c_rope).then_inc(rope_in, 16)
                        else:
                            sp.wait_ge(st_ready, hd)
                        sp.dma_start(decay[:, :], c_decay[ds(hd * P, P), :]).then_inc(decay_in, 16)

            head_chunks(0, m_heads, True)
            with sp.Fori(1, HEADS) as hd:
                head_chunks(hd, m_heads + 6 * hd, False)
            load_stack(HEADS - 1, 7, False)

            def merge(n, m, first):
                if first:
                    column_block(m, 0, w, C_GA + n * COLS)
                    column_block(m, 8, ret_w_o[0], n * COLS)
                else:
                    column_block(m, 0, ret_w_o[0], n * COLS)
                    column_block(m, 8, w, C_GA + n * COLS)
                column_block(m, 16, w, C_GB + n * COLS)
                column_block(m, 24, s5_glu_v[0], n * COLS, 4)
                column_block(m, 28, s5_glu_g[0], n * COLS, 4)

            merge(0, m_merge, True)
            with sp.Fori(1, NBLK) as n:
                merge(n, m_merge + 8 * n, False)
            with sp.Fori(0, NBLK) as n:
                column_block(m_wout + 2 * n, 0, w_out[0], n * COLS)
            with sp.Fori(0, HEADS) as hd:
                m = m_xattn + 6 * hd
                column_block(m, 0, xattn_wk[0], hd * COLS)
                column_block(m, 8, xattn_wq[0], hd * COLS)
                column_block(m, 16, xattn_wv[0], hd * COLS)
            with sp.Fori(0, NBLK) as n:
                column_block(m_wo + 2 * n, 0, xattn_wo[0], n * COLS)
            ffn(1)
            for t, b0, b1, scaled, count in ((0, 0, 1, scaled_v, 1), (0, 1, 2, scaled_v, 2),
                                             (1, 0, 3, scaled_s, 1), (0, 2, 4, scaled_v, 4),
                                             (1, 3, 4, scaled_v, 5)):
                sp.wait_ge(scaled, count)
                sp.dma_start(out[0, tok(t), b0 * COLS:b1 * COLS],
                             h[:, t, b0 * COLS:b1 * COLS]).then_inc(out_done, 16)
            sp.wait_ge(out_done, 16 * 5)

        @block.scalar
        def _(act):
            def split_hi(m, c, doubles=0):
                act.wait_ge(raw_in[c % SLOTS], 16 * (m + c // SLOTS + 1 + doubles))
                if not (isinstance(m, int) and 4 * m + c < SLOTS):
                    act.wait_ge(chunk_used, 4 * m + c - SLOTS + 1)
                act.activation(w_hi[:, c % SLOTS, :, :], raw[:, c % SLOTS, :, :],
                               ACT.Copy).then_inc(hi_done, 1)

            def evacuate(dst, pair, scale, done, func=ACT.Copy):
                for t in range(2):
                    i = act.activation(dst[:, t, :], acc[:, pair + t, :], func,
                                       scale=1.0 if scale is None else scale[:, t:t + 1])
                i.then_inc(done, 1)

            def block_split(b, gain, kt, src=tpk):
                act.wait_ge(blk_ps, b + 1)
                for j in range(4):
                    i = act.activation(xt_hi[:, ds(kt + j, 1), :], src[:, j:j + 1, :], ACT.Copy,
                                       scale=vecs[:, ds(gain + kt + j, 1)])
                i.then_inc(blk_hi, 1)

            def input_half(ps, done, kts):
                act.wait_ge(ps, 1)
                for kt in kts:
                    i = act.activation(xt_hi[:, kt, :], tpk[:, kt, :], ACT.Copy,
                                       scale=vecs[:, G_FFN1 + kt:G_FFN1 + kt + 1])
                i.then_inc(done, 1)

            def block_squares(src, n, unused):
                for t in range(2):
                    act.drain()
                    i = act.activation(unused[:, :], src[:, t, :], ACT.Square,
                                       accum_out=sumsq[:, t, ds(n, 1)])
                i.then_inc(sq_done, 1)

            def block_hi(b, gain, kt, src, n):
                block_split(b, gain, kt)
                block_squares(src, n, junk if b < 8 else junk2)

            def h_cols(n):
                return h[:, :, n * COLS:(n + 1) * COLS]

            def ffn(f):
                m0 = ffn_parts[f][0]
                scale = rstd[ffn_parts[f][4]]

                def silu_gate(m, s):
                    act.wait_ge(chunk_used, 4 * m + 8)
                    evacuate(gate, 0, scale, gate_ready[f], ACT.Silu)

                def hidden_hi(s, dst=ht_hi[:, :, :]):
                    act.wait_ge(hid_ps[f], s + 1)
                    act.activation(dst, tpk, ACT.Copy).then_inc(ht_h[f], 1)

                doubles = DOUBLES * f
                for c in range(16):
                    split_hi(m0, c, doubles)
                    if f == 0 and c == 0:
                        input_half(blk_ps, blk_hi, (2, 3))
                    if f == 0 and c in (2, 3, 5):
                        n = (c + 1) // 2
                        block_split(n, G_FFN1, 4 * n, input_banks[n])
                    if f == 0 and 5 < c < 10:
                        block_squares(h_cols(c - 6), c - 6, junk)
                    if f == 0 and c == 11:
                        vectors_and_parameters()
                    if f == 0 and c == 13:
                        s5_step_size()
                    if f == 1 and c == 4:
                        block_hi(15, G_FFN2, 12, nat, 3)
                    if f == 1 and c == 6:
                        copy_h(3, 12)
                    if c == (12 if f == 0 else 10):
                        act.wait_ge(rstd_ready, 1 if f == 0 else 4)
                        silu_gate(m0, 0)
                with act.Fori(1, LAST) as s:
                    m = m0 + 4 + 6 * (s - 1)
                    for c in range(24):
                        split_hi(m, c, doubles)
                        if c == 6:
                            hidden_hi(s - 1)
                        if c == 10:
                            silu_gate(m, s)
                m = m0 + 4 + 6 * (LAST - 1)
                for c in range(24):
                    split_hi(m, c, doubles)
                    if c == 6:
                        hidden_hi(LAST - 1)
                    if c == 10:
                        silu_gate(m, LAST)
                    if f == 0 and c == 14:
                        s5_trig()
                    if c == 22:
                        hidden_hi(LAST, yt_hi[:, 0:4, :])
                m += 6
                for c in range(8):
                    split_hi(m, c, doubles)
                    if f == 0 and c == 6:
                        block_hi(4, G_MIX, 0, h_cols(0), 0)
                    if f == 1 and c in (5, 7):
                        n = (c - 5) // 2
                        act.wait_ge(h_added[1], 4 * LAST + n + 1)
                        block_squares(h_cols(n), n, junk)

            def vectors_and_parameters():
                act.wait_ge(vecs_ps, 1)
                act.activation(vecs[:, KT:VROWS], tp[:, 0, KT:VROWS], ACT.Copy)
                act.activation(par[:, 0:3, :].rearrange("p a b -> p (a b)"), tp[:, 1, 0:96],
                               ACT.Copy).then_inc(par_ready, 1)

            def s5_step_size():
                act.wait_ge(par_ready, 1)
                act.activation(par[:, 3, :], par[:, 2, :], ACT.Exp).then_inc(exp_dt, 1)

            def s5_trig():
                act.wait_ge(angles, 1)
                act.activation(mag[:, :], par[:, 4, :], ACT.Exp)
                act.activation(par[:, 9, :], par[:, 7, :], ACT.Sin, scale=0.5)
                act.activation(par[:, 10, :], par[:, 7, :], ACT.Sin).then_inc(trig, 1)

            def copy_h(n, b0):
                act.wait_ge(hb_ready, 2 * (b0 - 8 + n) + 2)
                act.activation(h[:, :, ds(n * COLS, COLS)], nat[:, :, :], ACT.Copy)

            act.wait_ge(gain_ps, 1)
            act.activation(vecs[:, 0:KT], acc[:, 4, 0:KT], ACT.Copy).then_inc(gain_ready, 1)
            act.wait_ge(gain_ready, 1)
            input_half(x0_ps, x0_hi, (0, 1))
            ffn(0)

            for c in range(16):
                split_hi(m_mix, c)
                if c in (1, 3, 5):
                    n = (c + 1) // 2
                    block_split(4 + n, G_MIX, 4 * n)
                    if n < 3:
                        block_squares(h_cols(n), n, junk)
                if c == 8:
                    block_squares(h_cols(3), 3, junk)
                if 6 <= c < 14:
                    g = c - 6
                    act.wait_ge(bc_ps, g + 1)
                    dst = (b_t if g < 4 else c_t)[:, (g // 2) % 2, 4 * (g % 2):4 * (g % 2) + 4, :]
                    act.activation(dst.rearrange("p a b -> p (a b)"), acc[:, 4 + g % 2, :],
                                   ACT.Copy).then_inc(bc_ready, 1)
                if c == 11:
                    act.wait_ge(rstd_ready, 2)
                    act.wait_ge(chunk_used, 4 * m_mix + 8)
                    evacuate(nat, 2, rstd[1], u_nat)

            def values(hd, m):
                for t in range(2):
                    act.wait_ge(chunk_used if t else v_tile0, 4 * m if t else hd + 1)
                    act.activation(v_r[:, t, :], acc[:, 2 + t, :], ACT.Copy,
                                   scale=rstd[1][:, t:t + 1]).then_inc(v_ready, 1)

            def stage_b(q):
                act.activation(bu_parts[:, 0, :], b_t[:, :, ds(q, 1), :].rearrange("p r o s -> p r (o s)"),
                               ACT.Copy)
                act.activation(bu_parts[:, 2, :], u_t[:, ds(q, 1), :].rearrange("p o s -> p (o s)"),
                               ACT.Copy).then_inc(b_staged, 1)

            def stage_c(q):
                act.activation(c_st[:, :, :], c_t[:, :, ds(q, 1), :].rearrange("p r o s -> p r (o s)"),
                               ACT.Copy).then_inc(c_staged, 1)

            def group_scale(hd):
                act.wait_ge(grstd_ready, hd + 1)
                act.wait_ge(og_ready, hd + 1)
                for t in range(2):
                    i = act.activation(on[:, t, :], on[:, t, :], ACT.Copy, scale=grstd[:, t:t + 1])
                i.then_inc(on_ready, 1)

            def retention_hi(hd):
                act.wait_ge(on_ps, hd + 1)
                act.activation(yt_hi[:, ds(4 * hd, 4), :], tpk, ACT.Copy).then_inc(on_hi, 1)

            def head(hd, m, first):
                for c in range(24):
                    split_hi(m, c, 2 * hd + min(c // SLOTS + 1, 2))
                    if c == 0:
                        if first:
                            act.wait_ge(bc_ready, 8)
                            act.wait_ge(u_ready, 1)
                        else:
                            for i in range(2):
                                act.wait_ge(stack_in[i], 48 * 4 * hd)
                        stage_b(2 * hd)
                    if c == 1 and not first:
                        values(hd - 1, m)
                    if c == 2 and first:
                        act.wait_ge(chunk_used, 4 * m)
                        act.wait_ge(u_ps, 1)
                        evacuate(nat, 0, rstd[1], u_nat)
                    if c == 6:
                        if not first:
                            act.wait_ge(y_done, 8 * hd)
                        stage_c(2 * hd)
                        if not first:
                            group_scale(hd - 1)
                    if c == 9 and not first:
                        retention_hi(hd - 1)
                    if c == 10:
                        act.wait_ge(chunk_used, 4 * m + 8)
                        if first:
                            act.wait_ge(u_ps, 2)
                        evacuate(nat, 2, rstd[1], qk_nat)
                    if c == 12:
                        for i in range(2):
                            act.wait_ge(stack_in[i], 48 * (4 * hd + 2))
                        stage_b(2 * hd + 1)
                    if c == 17:
                        act.wait_ge(qk_ps, hd + 1)
                        act.activation(qk_t[:, :, :], tpk, ACT.Copy).then_inc(qk_ready, 1)
                    if c == 18:
                        act.wait_ge(y_done, 8 * hd + 4)
                        stage_c(2 * hd + 1)
                        act.wait_ge(chunk_used, 4 * m + 16)
                        evacuate(g_r, 0, rstd[1], g_ready, ACT.Silu)

            head(0, m_heads, True)
            with act.Fori(1, HEADS) as hd:
                head(hd, m_heads + 6 * hd, False)

            def glu_gate(n, m):
                act.wait_ge(chunk_used, 4 * m)
                evacuate(sg, 4, None, sg_ready, ACT.Sigmoid)

            def merged_hi(n):
                act.wait_ge(mg_ps, n + 1)
                act.activation(mt_hi[:, ds(4 * n, 4), :], tpk, ACT.Copy).then_inc(mg_hi, 1)

            def merge(n, m, first):
                for c in range(32):
                    split_hi(m, c, DOUBLES)
                    if c == 1:
                        if first:
                            values(HEADS - 1, m)
                        else:
                            glu_gate(n - 1, m)
                    if first and c == 6:
                        group_scale(HEADS - 1)
                    if first and c == 9:
                        retention_hi(HEADS - 1)
                    if not first and c == 5:
                        merged_hi(n - 1)
                    if c == (10 if first else 18):
                        act.wait_ge(chunk_used, 4 * m + c - 2)
                        evacuate(ga, 0 if first else 2, rstd[1], ga_ready, ACT.Sigmoid)
                    if first and c == 12:
                        act.wait_ge(y_out, QT)
                        act.activation(u_t[:, :, :], u_t[:, :, :],
                                       ACT.Gelu_apprx_tanh).then_inc(gelu_done, 1)
                    if first and c == 13:
                        act.wait_ge(gelu_done, 1)
                        act.activation(gl_hi[:, :, :], u_t[:, :, :], ACT.Copy).then_inc(gl_h, 1)
                    if c == (18 if first else 10):
                        act.wait_ge(chunk_used, 4 * m + c - 2)
                        evacuate(yb, 2 if first else 0, None, yb_ready)
                    if c == 26:
                        act.wait_ge(chunk_used, 4 * m + 24)
                        evacuate(gb, 0, rstd[1], gb_ready, ACT.Sigmoid)

            merge(0, m_merge, True)
            with act.Fori(1, NBLK) as n:
                merge(n, m_merge + 8 * n, False)

            def memory_hi(n):
                act.wait_ge(mem_ps, n + 1)
                for j in range(4):
                    i = act.activation(yt_hi[:, ds(4 * n + j, 1), :], tpk[:, j:j + 1, :],
                                       ACT.Copy, scale=vecs[:, ds(G_MEM + 4 * n + j, 1)])
                i.then_inc(mem_hi, 1)
                for t in range(2):
                    act.drain()
                    i = act.activation(junk2[:, :], memb[:, t, :], ACT.Square,
                                       accum_out=sumsq_mem[:, t, ds(n, 1)])
                i.then_inc(sqm_done, 1)

            def mixer_projection(n, m, first):
                for c in range(8):
                    split_hi(m, c, DOUBLES)
                    if first and c == 1:
                        glu_gate(NBLK - 1, m)
                    if first and c == 5:
                        merged_hi(NBLK - 1)
                    if not first and c == 2:
                        memory_hi(n - 1)
                    if not first and c == 4:
                        copy_h(n - 1, 8)
                    if not first and c == 6:
                        block_hi(8 + n - 1, G_X, 4 * (n - 1), nat, n - 1)

            mixer_projection(0, m_wout, True)
            with act.Fori(1, NBLK) as n:
                mixer_projection(n, m_wout + 2 * n, False)

            def attn_values(hd, m):
                act.wait_ge(chunk_used, 4 * m)
                evacuate(vx_hi, 4, rstd_mem, vx_h)

            def attn_hi(hd):
                act.wait_ge(xo_ps, hd + 1)
                act.activation(mt_hi[:, ds(4 * hd, 4), :], tpk, ACT.Copy).then_inc(xo_hi, 1)

            def attn_head(hd, m, first):
                for c in range(24):
                    split_hi(m, c, DOUBLES)
                    if c == 1 and not first:
                        attn_values(hd - 1, m)
                    if c == 2 and first:
                        memory_hi(NBLK - 1)
                    if c == 4 and not first:
                        attn_hi(hd - 1)
                    if c == 4 and first:
                        copy_h(3, 8)
                    if c == 6 and first:
                        block_hi(11, G_X, 12, nat, 3)
                    if c == 10:
                        act.wait_ge(chunk_used, 4 * m + 8)
                        act.wait_ge(rstdm_ready, 1)
                        evacuate(nat, 0, rstd_mem, kn_ready)
                    if c == 13:
                        act.wait_ge(kx_ps, hd + 1)
                        act.activation(kx_hi[:, :, :], tpk, ACT.Copy).then_inc(kx_h, 1)
                    if c == 17:
                        act.wait_ge(chunk_used, 4 * m + 16)
                        act.wait_ge(rstd_ready, 3)
                        evacuate(nat, 2, rstd[2], qn_ready)
                    if c == 19:
                        act.wait_ge(qx_ps, hd + 1)
                        act.activation(qx_hi[:, :, :], tpk, ACT.Copy).then_inc(qx_h, 1)
                    if c == 21:
                        act.wait_ge(nmax_ready, hd + 1)
                        for t in range(2):
                            i = act.activation(prob[:, t, :], tpk[:, t, :], ACT.Exp, scale=XSCALE,
                                               bias=nmax[:, t:t + 1], accum_out=rowsum[:, t:t + 1])
                        i.then_inc(exp_ready, 1)
                    if c == 23:
                        act.wait_ge(pt_ps, hd + 1)
                        act.activation(pt_hi[:, :, :], tpk[:, 2:4, :], ACT.Copy).then_inc(pt_h, 1)

            attn_head(0, m_xattn, True)
            with act.Fori(1, HEADS) as hd:
                attn_head(hd, m_xattn + 6 * hd, False)

            def attn_projection(n, m, first):
                for c in range(8):
                    split_hi(m, c, DOUBLES)
                    if first and c == 1:
                        attn_values(HEADS - 1, m)
                    if first and c == 4:
                        attn_hi(HEADS - 1)
                    if not first and c == 3:
                        copy_h(n - 1, 12)
                    if not first and c == 4:
                        block_hi(12 + n - 1, G_FFN2, 4 * (n - 1), nat, n - 1)

            attn_projection(0, m_wo, True)
            with act.Fori(1, NBLK) as n:
                attn_projection(n, m_wo + 2 * n, False)
            ffn(1)
            act.wait_ge(h_added[1], 4 * LAST + 3)
            block_squares(h_cols(2), 2, junk)
            for t in range(2):
                act.wait_ge(h_added[1], 4 * LAST + 4 + t)
                if t:
                    act.drain()
                i = act.activation(junk[:, :], h[:, t, 3 * COLS:], ACT.Square,
                                   accum_out=sumsq[:, t, 3:4])
            i.then_inc(sq_done, 1)
            act.wait_ge(gfin_used, 3)
            act.wait_ge(rstd_ready, 5)
            act.activation(h[:, 1, 0:3 * COLS], h[:, 1, 0:3 * COLS], ACT.Copy,
                           scale=rstd[4][:, 1:2]).then_inc(scaled_s, 1)

        @block.vector
        def _(dve):
            def split_lo(m, c):
                dve.wait_ge(hi_done, 4 * m + c + 1)
                dve.tensor_tensor(w_lo[:, c % SLOTS, :, :], raw[:, c % SLOTS, :, :],
                                  w_hi[:, c % SLOTS, :, :].bitcast(F32),
                                  ALU.subtract).then_inc(lo_done, 1)

            def input_half(done_hi, done, kts):
                dve.wait_ge(done_hi, 1)
                for kt in kts:
                    i = dve.scalar_tensor_tensor(
                        out=xt_lo[:, kt, :], in0=tpk[:, kt, :],
                        scalar=vecs[:, G_FFN1 + kt:G_FFN1 + kt + 1],
                        in1=xt_hi[:, kt, :].bitcast(F32), op0=ALU.mult, op1=ALU.subtract)
                i.then_inc(done, 1)

            def block_lo(b, gain, kt, src=tpk):
                dve.wait_ge(blk_hi, b + 1)
                for j in range(4):
                    i = dve.scalar_tensor_tensor(
                        out=xt_lo[:, ds(kt + j, 1), :], in0=src[:, j:j + 1, :],
                        scalar=vecs[:, ds(gain + kt + j, 1)],
                        in1=xt_hi[:, ds(kt + j, 1), :].bitcast(F32), op0=ALU.mult, op1=ALU.subtract)
                i.then_inc(blk_lo, 1)

            def mean_square(sums, mean, ready, sums_done, count):
                dve.wait_ge(sums_done, count)
                dve.tensor_reduce(mean[:, :], sums[:, :, :], AX_X, ALU.add)
                dve.drain()
                dve.tensor_scalar(mean[:, :], mean[:, :], 1.0 / D, RMS_EPS, ALU.mult,
                                  ALU.add).then_inc(ready, 1)

            def lo_of(dst_hi, dst_lo, done_hi, count, done):
                dve.wait_ge(done_hi, count)
                dve.tensor_tensor(dst_lo, tpk, dst_hi.bitcast(F32), ALU.subtract).then_inc(done, 1)

            def ffn(f):
                m0 = ffn_parts[f][0]
                scale = rstd[ffn_parts[f][4]]

                def hidden(m, s):
                    dve.wait_ge(chunk_used, 4 * m)
                    dve.wait_ge(gate_ready[f], s + 1)
                    for t in range(2):
                        i = dve.scalar_tensor_tensor(out=hid[:, t, :], in0=acc[:, 2 + t, :],
                                                     scalar=scale[:, t:t + 1], in1=gate[:, t, :],
                                                     op0=ALU.mult, op1=ALU.mult)
                    i.then_inc(hid_ready[f], 1)

                def add_half(m, c, n, pairs=(4, 2, 4, 0)):
                    dve.wait_ge(chunk_used, 4 * m + c + 1)
                    pair = pairs[n]
                    for t in range(2):
                        hb = h[:, t, n * COLS:(n + 1) * COLS]
                        i = dve.scalar_tensor_tensor(out=hb, in0=acc[:, pair + t, :], scalar=0.5,
                                                     in1=hb, op0=ALU.mult, op1=ALU.add)
                    i.then_inc(h_added[f], 1)

                for c in range(16):
                    split_lo(m0, c)
                    if f == 0 and c == 0:
                        input_half(blk_hi, blk_lo, (2, 3))
                    if f == 0 and c in (2, 3, 5):
                        n = (c + 1) // 2
                        block_lo(n, G_FFN1, 4 * n, input_banks[n])
                    if f == 0 and c == 4:
                        step_rows()
                    if f == 0 and c == 10:
                        mean_square(sumsq, meansq, ms_ready, sq_done, 4)
                    if f == 1 and c == 1:
                        add_block(NBLK - 1, m0, 8)
                    if f == 1 and c == 4:
                        block_lo(15, G_FFN2, 12)
                    if f == 1 and c == 5:
                        mean_square(sumsq, meansq, ms_ready, sq_done, 16)
                with dve.Fori(1, LAST) as s:
                    m = m0 + 4 + 6 * (s - 1)
                    for c in range(24):
                        split_lo(m, c)
                        if c == 3:
                            hidden(m, s - 1)
                        if c == 6:
                            lo_of(ht_hi[:, :, :], ht_lo[:, :, :], ht_h[f], s, ht_l[f])
                        if c in (12, 14, 16, 18):
                            add_half(m, c - 3, (c - 12) // 2)
                m = m0 + 4 + 6 * (LAST - 1)
                other_pairs = (4, 0, 4, 2)
                for c in range(24):
                    split_lo(m, c)
                    if c == 3:
                        hidden(m, LAST - 1)
                    if c == 6:
                        lo_of(ht_hi[:, :, :], ht_lo[:, :, :], ht_h[f], LAST, ht_l[f])
                    if c == 18:
                        hidden(m + 4, LAST)
                    if c in (20, 21):
                        add_half(m, 17 + 2 * (c - 20), c - 20, other_pairs)
                    if c == 22:
                        lo_of(yt_hi[:, 0:4, :], yt_lo[:, 0:4, :], ht_h[f], SUPER, ht_l[f])
                for c in range(8):
                    split_lo(m + 6, c)
                    if c in (0, 1):
                        add_half(m, 21 + 2 * c, 2 + c, other_pairs)
                    if c in (3, 5, 7):
                        add_half(m + 6, c - 2, (c - 3) // 2)
                    if f == 0 and c == 6:
                        block_lo(4, G_MIX, 0)
                    if f == 1 and c in (6, 7):
                        apply_gain(c - 6)
                return add_half

            def apply_gain(n):
                if n == 0:
                    dve.wait_ge(gfin_in, 16)
                dve.wait_ge(sq_done, 16 + n + 1)
                g = gfin[:, n * COLS:(n + 1) * COLS].unsqueeze(1).broadcast_to([P, 2, COLS])
                hb = h[:, :, n * COLS:(n + 1) * COLS]
                dve.tensor_tensor(hb, hb, g, ALU.mult).then_inc(gfin_used, 1)

            def step_rows():
                dve.wait_ge(par_in, 48)
                dve.tensor_copy(prow[64:96, :].rearrange("p (g s) -> p g s", g=2),
                                dt_row[64:96, :].unsqueeze(2).broadcast_to([PAIRS, 2, 64])
                                ).then_inc(dt_rows, 1)

            dve.memset(mhalf[:, :], -0.5)
            input_half(x0_hi, x0_lo, (0, 1))
            add_half = ffn(0)

            m_tail = m_mix - 2
            for c in range(16):
                split_lo(m_mix, c)
                if c == 1:
                    add_half(m_tail, 7, 3)
                if c in (1, 3, 5):
                    block_lo(4 + (c + 1) // 2, G_MIX, 2 * (c + 1))
                if c == 9:
                    mean_square(sumsq, meansq, ms_ready, sq_done, 8)
                if c == 15:
                    dve.wait_ge(u_ps, 1)
                    dve.tensor_copy(u_t[:, 0:4, :], tpk).then_inc(u_ready, 1)

            def rotate_and_scan(hd, p, first):
                buf = p % 2
                dve.wait_ge(bu_done, 8 * hd + p + 1)
                dve.wait_ge(tab_ready, 8 * hd + p + 1)
                if not (first and p in (0, 1)):
                    dve.wait_ge(s_ready, 8 * hd + p - 1)
                z = zb[:, buf, :, :]
                dve.tensor_tensor(z, s5_in, tab[:, buf, 0:1, :].broadcast_to([P, 2, SEQ]), ALU.mult)
                dve.tensor_tensor(rot2[:, :, :], s5_in, tab[:, buf, 1:2, :].broadcast_to([P, 2, SEQ]),
                                  ALU.mult).then_inc(x_free, 1)
                dve.drain()
                dve.tensor_tensor(zb[:, buf, 0, :], zb[:, buf, 0, :], rot2[:, 1, :], ALU.add)
                dve.tensor_tensor(zb[:, buf, 1, :], zb[:, buf, 1, :], rot2[:, 0, :], ALU.subtract)
                dve.drain()
                r = mag[:, ds(8 * hd + p, 1)].broadcast_to([P, SEQ])
                for part in range(2):
                    i = dve.tensor_tensor_scan(zb[:, buf, part, :], r, zb[:, buf, part, :], 0.0,
                                               ALU.mult, ALU.add)
                i.then_inc(z_ready, 1)

            def split_b(q):
                dve.wait_ge(b_staged, q + 1)
                b = b_t[:, :, ds(q, 1), :].rearrange("p r o s -> p r (o s)")
                u = u_t[:, ds(q, 1), :].rearrange("p o s -> p (o s)")
                dve.tensor_tensor(bu_parts[:, 1, :], b, bu_parts[:, 0, :].bitcast(F32), ALU.subtract)
                dve.tensor_tensor(bu_parts[:, 3, :], u, bu_parts[:, 2, :].bitcast(F32),
                                  ALU.subtract).then_inc(b_split, 1)

            def add_skip(q):
                dve.wait_ge(y_done, 4 * q + 4)
                u = u_t[:, ds(q, 1), :].rearrange("p o s -> p (o s)")
                dve.scalar_tensor_tensor(out=u, in0=u, scalar=vecs[:, ds(G_D + q, 1)], in1=s5_out,
                                         op0=ALU.mult, op1=ALU.add).then_inc(y_out, 1)

            def group_stats(hd):
                dve.wait_ge(pv_ps, hd + 1)
                for t in range(2):
                    dve.bn_stats(bstat[:, t, :], tp[:, t, :])
                dve.drain()
                for t in range(2):
                    dve.bn_aggr(mv[:, t, :], bstat[:, t, :])
                dve.drain()
                dve.tensor_scalar(vare[:, :], mv[:, :, 1], GN_EPS, None,
                                  ALU.add).then_inc(var_ready, 1)

            def group_gate(hd):
                dve.wait_ge(g_ready, hd + 1)
                for t in range(2):
                    i = dve.scalar_tensor_tensor(out=on[:, t, :], in0=tp[:, t, :],
                                                 scalar=mv[:, t, 0:1], in1=g_r[:, t, :],
                                                 op0=ALU.subtract, op1=ALU.mult)
                i.then_inc(og_ready, 1)

            def rotary(hd, t):
                dve.wait_ge(qk_nat, hd + 1)
                src = nat[:, t, :].rearrange("p (a d) -> p a d", d=P)
                for s in range(2):
                    dve.tensor_tensor(on[:, s, :].rearrange("p (a d) -> p a d", d=P), src,
                                      rope[:, t, s:s + 1, :].broadcast_to([P, 4, P]), ALU.mult)
                dve.drain()
                dst = nat[:, t, :].rearrange("p (a f d) -> p a f d", a=2, f=2)
                cos = on[:, 0, :].rearrange("p (a f d) -> p a f d", a=2, f=2)
                sin = on[:, 1, :].rearrange("p (a f d) -> p a f d", a=2, f=2)
                dve.tensor_tensor(dst[:, :, 0, :], cos[:, :, 0, :], sin[:, :, 1, :], ALU.subtract)
                dve.tensor_tensor(dst[:, :, 1, :], cos[:, :, 1, :], sin[:, :, 0, :],
                                  ALU.add).then_inc(rot_ready, 1)

            def retention_lo(hd):
                lo_of(yt_hi[:, ds(4 * hd, 4), :], yt_lo[:, ds(4 * hd, 4), :], on_hi, hd + 1, on_lo)

            def head(hd, m, first):
                for c in range(24):
                    split_lo(m, c)
                    if c in (0, 12):
                        split_b(2 * hd + c // 12)
                    if c % 3 == 0 and not (first and c == 0):
                        rotate_and_scan(hd, c // 3 - 1, first)
                    if not first and c == 2:
                        group_stats(hd - 1)
                    if not first and c == 4:
                        group_gate(hd - 1)
                    if not first and c == 5:
                        add_skip(2 * hd - 1)
                    if c == 6 and first:
                        dve.wait_ge(u_ps, 2)
                        dve.tensor_copy(u_t[:, 4:8, :], tpk).then_inc(u_ready, 1)
                    if c == 10 and not first:
                        retention_lo(hd - 1)
                    if c == 11:
                        if first:
                            dve.wait_ge(rope_in, 16)
                        rotary(hd, 0)
                    if c == 13:
                        dve.drain()
                        rotary(hd, 1)
                    if c == 17:
                        add_skip(2 * hd)
                    if c == 20:
                        dve.wait_ge(st_ps, hd + 1)
                        dve.wait_ge(decay_in, 16 * (hd + 1))
                        dve.tensor_tensor(s_t0[:, :], tp[:, 0, 0:SEQ], decay[:, 0:SEQ], ALU.mult)
                        dve.tensor_tensor(s_t1[:, :], tp[:, 0, 384:512], decay[:, SEQ:384],
                                          ALU.mult).then_inc(st_ready, 1)

            head(0, m_heads, True)
            with dve.Fori(1, HEADS) as hd:
                head(hd, m_heads + 6 * hd, False)

            def add_branches(n):
                dve.wait_ge(sg_ready, n + 1)
                dve.tensor_tensor(ga[:, :, :], ga[:, :, :], sg[:, :, :], ALU.mult)
                dve.drain()
                dve.tensor_tensor(yb[:, :, :], yb[:, :, :], ga[:, :, :], ALU.add).then_inc(mg_ready, 1)

            def merged_lo(n):
                lo_of(mt_hi[:, ds(4 * n, 4), :], mt_lo[:, ds(4 * n, 4), :], mg_hi, n + 1, mg_lo)

            def merge(n, m, first):
                for c in range(32):
                    split_lo(m, c)
                    if first and c == 0:
                        rotate_and_scan(HEADS, -1, False)
                    if first and c == 2:
                        group_stats(HEADS - 1)
                    if first and c == 4:
                        group_gate(HEADS - 1)
                    if first and c == 6:
                        add_skip(QT - 1)
                    if first and c == 10:
                        retention_lo(HEADS - 1)
                    if not first and c == 2:
                        add_branches(n - 1)
                    if not first and c == 5:
                        merged_lo(n - 1)
                    if first and c == 16:
                        dve.wait_ge(gl_h, 1)
                        dve.tensor_tensor(gl_lo[:, :, :], u_t[:, :, :], gl_hi[:, :, :].bitcast(F32),
                                          ALU.subtract).then_inc(gl_l, 1)
                    if c == 28:
                        dve.wait_ge(gb_ready, n + 1)
                        dve.tensor_tensor(yb[:, :, :], yb[:, :, :], gb[:, :, :], ALU.mult)
                    if c == 30:
                        dve.wait_ge(chunk_used, 4 * m + 28)
                        for t in range(2):
                            i = dve.tensor_tensor(ga[:, t, :], acc[:, 2 + t, :], ga[:, t, :], ALU.mult)
                        i.then_inc(va_ready, 1)

            merge(0, m_merge, True)
            with dve.Fori(1, NBLK) as n:
                merge(n, m_merge + 8 * n, False)

            def add_block(n, m, b0):
                for t in range(2):
                    if t == 0:
                        dve.wait_ge(tile0_done, b0 + n + 1 - 4)
                    else:
                        dve.wait_ge(chunk_used, 4 * m)
                    dve.tensor_tensor(nat[:, t, :], acc[:, 2 + t, :],
                                      h[:, t, ds(n * COLS, COLS)], ALU.add).then_inc(hb_ready, 1)

            def memory_lo(n):
                dve.wait_ge(mem_hi, n + 1)
                for j in range(4):
                    kt = 4 * n + j
                    i = dve.scalar_tensor_tensor(
                        out=yt_lo[:, ds(kt, 1), :], in0=tpk[:, j:j + 1, :],
                        scalar=vecs[:, ds(G_MEM + kt, 1)], in1=yt_hi[:, ds(kt, 1), :].bitcast(F32),
                        op0=ALU.mult, op1=ALU.subtract)
                i.then_inc(mem_lo, 1)

            def mixer_projection(n, m, first):
                for c in range(8):
                    split_lo(m, c)
                    if first and c == 2:
                        add_branches(NBLK - 1)
                    if first and c == 5:
                        merged_lo(NBLK - 1)
                    if not first and c == 1:
                        add_block(n - 1, m, 4)
                    if not first and c == 2:
                        memory_lo(n - 1)
                    if not first and c == 6:
                        block_lo(8 + n - 1, G_X, 4 * (n - 1))

            mixer_projection(0, m_wout, True)
            with dve.Fori(1, NBLK) as n:
                mixer_projection(n, m_wout + 2 * n, False)

            def attn_lo(hd):
                lo_of(mt_hi[:, ds(4 * hd, 4), :], mt_lo[:, ds(4 * hd, 4), :], xo_hi, hd + 1, xo_lo)

            def attn_values(hd, m):
                dve.wait_ge(vx_h, hd + 1)
                for t in range(2):
                    i = dve.scalar_tensor_tensor(
                        out=vx_lo[:, t, :], in0=acc[:, 4 + t, :], scalar=rstd_mem[:, t:t + 1],
                        in1=vx_hi[:, t, :].bitcast(F32), op0=ALU.mult, op1=ALU.subtract)
                i.then_inc(vx_l, 1)

            def attn_head(hd, m, first):
                for c in range(24):
                    split_lo(m, c)
                    if not first and c == 1:
                        attn_values(hd - 1, m)
                    if c == 13:
                        lo_of(kx_hi[:, :, :], kx_lo[:, :, :], kx_h, hd + 1, kx_l)
                    if c == 19:
                        lo_of(qx_hi[:, :, :], qx_lo[:, :, :], qx_h, hd + 1, qx_l)
                    if c == 23:
                        dve.wait_ge(pt_h, hd + 1)
                        dve.tensor_tensor(pt_lo[:, :, :], tpk[:, 2:4, :],
                                          pt_hi[:, :, :].bitcast(F32),
                                          ALU.subtract).then_inc(pt_l, 1)
                    if first and c == 1:
                        add_block(NBLK - 1, m, 4)
                    if first and c == 2:
                        memory_lo(NBLK - 1)
                    if first and c == 4:
                        mean_square(sumsq_mem, meansq_mem, msm_ready, sqm_done, NBLK)
                    if first and c == 6:
                        block_lo(11, G_X, 12)
                    if first and c == 7:
                        mean_square(sumsq, meansq, ms_ready, sq_done, 12)
                    if not first and c == 4:
                        attn_lo(hd - 1)
                    if c == 21:
                        dve.wait_ge(sc_ps, hd + 1)
                        dve.tensor_reduce(smax[:, :], tpk[:, 0:2, :], AX_X, ALU.max)
                        dve.drain()
                        dve.tensor_scalar(nmax[:, :], smax[:, :], -XSCALE, None,
                                          ALU.mult).then_inc(nmax_ready, 1)
                    if c == 22:
                        dve.wait_ge(exp_ready, hd + 1)
                        dve.reciprocal(rinv[:, :], rowsum[:, :])
                        dve.drain()
                        for t in range(2):
                            i = dve.tensor_scalar(prob[:, t, :], prob[:, t, :], rinv[:, t:t + 1],
                                                  None, ALU.mult)
                        i.then_inc(prob_ready, 1)

            attn_head(0, m_xattn, True)
            with dve.Fori(1, HEADS) as hd:
                attn_head(hd, m_xattn + 6 * hd, False)

            def attn_projection(n, m, first):
                for c in range(8):
                    split_lo(m, c)
                    if first and c == 1:
                        attn_values(HEADS - 1, m)
                    if first and c == 4:
                        attn_lo(HEADS - 1)
                    if not first and c == 1:
                        add_block(n - 1, m, 8)
                    if not first and c == 4:
                        block_lo(12 + n - 1, G_FFN2, 4 * (n - 1))

            attn_projection(0, m_wo, True)
            with dve.Fori(1, NBLK) as n:
                attn_projection(n, m_wo + 2 * n, False)
            add_half = ffn(1)
            apply_gain(2)
            for t in range(2):
                if t == 0:
                    dve.wait_ge(tile0_done, 2 * NBLK + 1)
                else:
                    dve.wait_ge(chunk_used, 4 * (m_ffn2 + 6 + 6 * LAST))
                hb = h[:, t, 3 * COLS:]
                dve.scalar_tensor_tensor(out=hb, in0=acc[:, t, :], scalar=0.5, in1=hb,
                                         op0=ALU.mult, op1=ALU.add).then_inc(h_added[1], 1)
            mean_square(sumsq, meansq, ms_ready, sq_done, 20)
            apply_gain(3)
            dve.wait_ge(rstd_ready, 5)
            for t, n in ((0, 0), (0, 1), (0, 2), (0, 3), (1, 3)):
                if n == 3:
                    dve.wait_ge(gfin_used, 4)
                hb = h[:, t, n * COLS:(n + 1) * COLS]
                dve.tensor_scalar(hb, hb, rstd[4][:, t:t + 1], None,
                                  ALU.mult).then_inc(scaled_v, 1)

        @block.tensor
        def _(pe):
            def product(o, a, b, start, stop):
                pe.matmul(o, a[0], b[0], start=start, stop=False)
                pe.matmul(o, a[0], b[1], start=False, stop=False)
                return pe.matmul(o, a[1], b[0], start=False, stop=stop)

            def chunk(m, c, hi, lo, kt, pair, first, last, tile_free=None,
                      tile0=None):
                pe.wait_ge(lo_done, 4 * m + c + 1)
                s = c % SLOTS
                for t in range(2):
                    if first and tile_free:
                        tile_free(t)
                    o = acc[:, pair + t, :]
                    for k in range(2):
                        i = product(o, (hi[:, kt + k, tok(t)], lo[:, kt + k, tok(t)]),
                                    (w_hi[:, s, k, :], w_lo[:, s, k, :]),
                                    first and k == 0, last and k == 1)
                    if t == 0 and last and tile0:
                        i.then_inc(tile0, 1)
                i.then_inc(chunk_used, 1)

            def transpose_block(src, done):
                for j in range(4):
                    for t in range(2):
                        i = pe.transpose(tpk[:, j, tok(t)], src[:, t, j * P:(j + 1) * P], ident[:, :])
                i.then_inc(done, 1)

            def column_block(m, c0, hi, lo, pair, after=None, chunks=8, before=None,
                             tile_free=None, tile0=None):
                for c in range(chunks):
                    if before:
                        before(c0 + c)
                    chunk(m, c0 + c, hi, lo, 2 * c, pair, c == 0, c == chunks - 1,
                          tile_free, tile0)
                    if after:
                        after(c0 + c)

            def turn_h(n, b0):
                pe.wait_ge(hb_ready, 2 * (b0 - 8 + n) + 2)
                pe.wait_ge(blk_lo, b0 + n)
                transpose_block(nat, blk_ps)

            def ffn(f):
                m0 = ffn_parts[f][0]

                def down(m, c0, a_hi, a_lo, pairs, before, after=None, tile0=None):
                    for c in range(8):
                        before(c)
                        chunk(m, c0 + c, a_hi, a_lo, 2 * (c % 2), pairs[c // 2],
                              c % 2 == 0, c % 2 == 1, tile0=tile0 if c == 7 else None)
                        if after:
                            after(c)

                def first_before(c):
                    if f == 0 and c == 0:
                        pe.wait_ge(x0_lo, 1)
                    elif f == 0 and c == 1:
                        pe.wait_ge(blk_lo, 1)
                    elif c % 2 == 0:
                        pe.wait_ge(blk_lo, (0 if f == 0 else 12) + c // 2 + 1)

                def first_after(c):
                    if f == 0 and c < 3:
                        turn_input(c + 1, x_in[c + 1], range(4 * c + 4, 4 * c + 8))
                    if f == 0 and c == 9:
                        turn_parameters()
                    if f == 1 and c == 1:
                        turn_h(3, 12)

                column_block(m0, 0, xt_hi, xt_lo, 0, first_after, before=first_before)
                column_block(m0, 8, xt_hi, xt_lo, 2, first_after)

                def first_product(m, s):
                    def turn_hidden(c):
                        if c == 3:
                            pe.wait_ge(hid_ready[f], s)
                            transpose_block(hid, hid_ps[f])

                    pe.wait_ge(gate_ready[f], s)
                    column_block(m, 0, xt_hi, xt_lo, 0, turn_hidden)

                with pe.Fori(1, LAST) as s:
                    m = m0 + 4 + 6 * (s - 1)
                    first_product(m, s)
                    pe.wait_ge(ht_l[f], s)

                    def banks_free(c):
                        if c == 4:
                            pe.wait_ge(h_added[f], 4 * s - 3)
                        if c == 6:
                            pe.wait_ge(gate_ready[f], s + 1)

                    down(m, 8, ht_hi, ht_lo, (4, 2, 4, 0), banks_free)
                    pe.wait_ge(h_added[f], 4 * s - 2)
                    column_block(m, 16, xt_hi, xt_lo, 2)
                    pe.wait_ge(h_added[f], 4 * s)

                m = m0 + 4 + 6 * (LAST - 1)
                first_product(m, LAST)
                column_block(m, 8, xt_hi, xt_lo, 2)
                pe.wait_ge(ht_l[f], LAST)

                def turn_last(c):
                    if c == 3:
                        pe.wait_ge(hid_ready[f], SUPER)
                        transpose_block(hid, hid_ps[f])

                def before_last_but_one(c):
                    if c == 2:
                        pe.wait_ge(gate_ready[f], SUPER)
                    if c == 4:
                        pe.wait_ge(h_added[f], 4 * LAST - 3)
                    if c == 6:
                        pe.wait_ge(hid_ready[f], SUPER)

                down(m, 16, ht_hi, ht_lo, (4, 0, 4, 2), before_last_but_one, turn_last)
                pe.wait_ge(ht_l[f], SUPER)

                def last_after(c):
                    if f == 0 and c in (3, 6):
                        turn_residual((c - 3) // 3)

                def before_last(c):
                    if c == 0:
                        pe.wait_ge(h_added[f], 4 * LAST - 1)
                    if c == 2:
                        pe.wait_ge(h_added[f], 4 * LAST)
                    if c == 4:
                        pe.wait_ge(h_added[f], 4 * LAST + 1)

                down(m + 6, 0, yt_hi, yt_lo, (4, 2, 4, 0), before_last, last_after,
                     tile0_done if f == 1 else None)

            def turn_residual(n):
                pe.wait_ge(h_added[0], 4 * LAST + n + 1)
                if n:
                    pe.wait_ge(blk_lo, 4 + n)
                transpose_block(h[:, :, n * COLS:(n + 1) * COLS], blk_ps)

            def turn_input(n, landed, kts, done=blk_ps):
                pe.wait_ge(landed, 16)
                if n == 3:
                    pe.wait_ge(blk_lo, 1)
                for kt in kts:
                    for t in range(2):
                        i = pe.transpose(input_banks[n][:, kt % 4, tok(t)],
                                         h[:, t, kt * P:(kt + 1) * P], ident[:, :])
                i.then_inc(done, 1)

            def turn_parameters():
                pe.wait_ge(vec_in, 80)
                pe.wait_ge(dt_rows, 1)
                pe.transpose(tp[:, 0, 0:VROWS], vrow[0:VROWS, :], ident[0:VROWS, 0:VROWS])
                pe.transpose(tp[:, 1, 0:96], prow[0:96, :], ident[0:96, 0:96]).then_inc(vecs_ps, 1)

            pe.wait_ge(ident_in, 16)
            pe.wait_ge(gain_in, 16)
            pe.transpose(acc[:, 4, 0:KT], vrow[0:KT, :], ident[0:KT, 0:KT]).then_inc(gain_ps, 1)
            turn_input(0, x0_in, (0, 1), x0_ps)
            turn_input(0, x_in[0], (2, 3))
            ffn(0)

            def mix_ready(c):
                if c < 8 and c % 2 == 0:
                    pe.wait_ge(blk_lo, 4 + c // 2 + 1)

            def mix_after(c):
                if c in (1, 3):
                    turn_residual(2 + c // 2)
                if 4 <= c < 12:
                    g = c - 4
                    if g == 0:
                        pe.wait_ge(pads_ready, 1)
                        pe.wait_ge(h_added[0], 4 * LAST + 3)
                    if g >= 2:
                        pe.wait_ge(bc_ready, g - 1)
                    for j in range(4):
                        q = 4 * (g % 2) + j
                        if g < 4:
                            src = b_pad[:, (g // 2) % 2, 4 * q:4 * q + 4, :].rearrange("p a b -> p (a b)")
                        else:
                            src = c_pad[:, (g // 2) % 2, q, :]
                        i = pe.transpose(acc[:, 4 + g % 2, j * P:(j + 1) * P], src, ident[:, :])
                    i.then_inc(bc_ps, 1)
                if c == 12:
                    pe.wait_ge(u_nat, 1)
                    pe.wait_ge(blk_lo, 8)
                    transpose_block(nat, u_ps)

            column_block(m_mix, 0, xt_hi, xt_lo, 2, mix_after, before=mix_ready)
            pe.wait_ge(h_added[0], 4 * LAST + 4)
            column_block(m_mix, 8, xt_hi, xt_lo, 0, mix_after)

            def c_product(hd, c, first):
                p = c // 3
                prev = p - 2
                if prev >= 0 or not first:
                    i4 = prev % 4
                    if prev in (0, 4):
                        pe.wait_ge(c_staged, 2 * hd + prev // 4 + 1)
                        if prev == 4 or not first:
                            pe.wait_ge(y_out, 2 * hd + prev // 4)
                    pe.wait_ge(s_ready, 8 * hd + p - 1)
                    o = acc[32 * i4:32 * i4 + 32, 5, 0:SEQ]
                    for part in range(2):
                        i = pe.matmul(o, c_st[:, part, 32 * i4:32 * i4 + 32],
                                      state[:, p % 2, part, :], start=part == 0, stop=part == 1)
                    i.then_inc(y_done, 1)

            def b_product(hd, p, first):
                pe.wait_ge(stack_in[p % 2], 48 * (4 * hd + p // 2 + 1))
                if not (first and p == 0):
                    pe.wait_ge(x_free, 8 * hd + p)
                for part in range(2):
                    i = pe.matmul(s5_in[:, part, :], bu_stack[p % 2][:, 0, part * P:(part + 1) * P],
                                  bu_stack[p % 2][:, 1, :], start=True, stop=True)
                i.then_inc(bu_done, 1)

            def retention_out(hd):
                pe.wait_ge(v_ready, 2 * hd + 2)
                pe.wait_ge(st_ready, hd + 1)
                pe.matmul(tp[:, 0, :], s_t0[:, tok(0)], v_r[:, 0, :], start=True, stop=True)
                pe.matmul(tp[:, 1, :], s_t0[:, tok(1)], v_r[:, 0, :], start=True, stop=False)
                pe.matmul(tp[:, 1, :], s_t1[:, :], v_r[:, 1, :], start=False,
                          stop=True).then_inc(pv_ps, 1)

            def head(hd, m, first):
                def after(c):
                    if c == 0 and not first:
                        retention_out(hd - 1)
                    if c % 3 == 0:
                        if c > 0:
                            c_product(hd, c, first)
                        b_product(hd, c // 3, first)
                    if first and c == 3:
                        pe.wait_ge(u_nat, 2)
                        pe.wait_ge(u_ready, 1)
                        transpose_block(nat, u_ps)
                    if not first and c == 6:
                        pe.wait_ge(on_ready, hd)
                        transpose_block(on, on_ps)
                    if c == 14:
                        pe.wait_ge(rot_ready, 2 * hd + 2)
                        if first:
                            pe.wait_ge(u_ready, 2)
                        else:
                            pe.wait_ge(on_lo, hd)
                        transpose_block(nat, qk_ps)
                    if c == 17:
                        pe.wait_ge(qk_ready, hd + 1)
                        for dt in range(2):
                            pe.matmul(tp[:, 0, 0:SEQ], qk_t[:, 2 + dt, tok(0)], qk_t[:, dt, :],
                                      start=dt == 0, stop=dt == 1)
                        for dt in range(2):
                            i = pe.matmul(tp[:, 0, 384:512], qk_t[:, 2 + dt, tok(1)],
                                          qk_t[:, dt, tok(1)], start=dt == 0, stop=dt == 1)
                        i.then_inc(st_ps, 1)

                def tile_free(t):
                    pe.wait_ge(v_ready, 2 * hd - 1 + t)

                if not first:
                    c_product(hd, 0, False)
                column_block(m, 0, xt_hi, xt_lo, 2, after, tile_free=None if first else tile_free)
                if first:
                    pe.wait_ge(u_nat, 2)
                else:
                    pe.wait_ge(g_ready, hd)
                column_block(m, 8, xt_hi, xt_lo, 0, after)
                pe.wait_ge(qk_nat, hd + 1)
                column_block(m, 16, xt_hi, xt_lo, 2, after, tile0=v_tile0)

            head(0, m_heads, True)
            with pe.Fori(1, HEADS) as hd:
                head(hd, m_heads + 6 * hd, False)

            def merge(n, m, first):
                def before(c):
                    if first and c == 14:
                        pe.wait_ge(on_lo, HEADS)

                def after(c):
                    if first and c == 0:
                        retention_out(HEADS - 1)
                    if first and c in (0, 3):
                        pe.wait_ge(s_ready, 31 + c // 3)
                        i4 = 2 + c // 3
                        o = acc[32 * i4:32 * i4 + 32, 5, 0:SEQ]
                        for part in range(2):
                            i = pe.matmul(o, c_st[:, part, 32 * i4:32 * i4 + 32],
                                          state[:, c // 3, part, :], start=part == 0, stop=part == 1)
                        i.then_inc(y_done, 1)
                    if first and c == 6:
                        pe.wait_ge(on_ready, HEADS)
                        transpose_block(on, on_ps)
                    if not first and c == 3:
                        pe.wait_ge(mg_ready, n)
                        transpose_block(yb, mg_ps)

                if first:
                    pe.wait_ge(g_ready, HEADS)
                else:
                    pe.wait_ge(gb_ready, n)
                if first:
                    column_block(m, 0, xt_hi, xt_lo, 0, after)
                    pe.wait_ge(v_ready, 2 * HEADS)
                    column_block(m, 8, yt_hi, yt_lo, 2, before=before)
                else:
                    column_block(m, 0, yt_hi, yt_lo, 0, after)
                    pe.wait_ge(va_ready, n)
                    column_block(m, 8, xt_hi, xt_lo, 2)
                pe.wait_ge(ga_ready if first else yb_ready, n + 1)
                column_block(m, 16, xt_hi, xt_lo, 0)
                pe.wait_ge(yb_ready if first else ga_ready, n + 1)
                if first:
                    pe.wait_ge(gl_l, 1)
                column_block(m, 24, gl_hi, gl_lo, 2, chunks=4)
                if first:
                    pe.wait_ge(y_out, QT)
                else:
                    pe.wait_ge(sg_ready, n)
                column_block(m, 28, gl_hi, gl_lo, 4, chunks=4)

            merge(0, m_merge, True)
            with pe.Fori(1, NBLK) as n:
                merge(n, m_merge + 8 * n, False)

            def turn_memory(n):
                pe.wait_ge(mem_in, 16 * (n + 1))
                transpose_block(memb, mem_ps)

            def mixer_projection(n, m, first):
                def before(c):
                    if first and c == 6:
                        pe.wait_ge(mg_lo, NBLK)

                def after(c):
                    if first and c == 3:
                        pe.wait_ge(mg_ready, NBLK)
                        transpose_block(yb, mg_ps)
                    if not first and c == 3:
                        pe.wait_ge(mem_lo, n)
                        turn_h(n - 1, 8)
                    if c == 7:
                        if not first:
                            pe.wait_ge(blk_lo, 8 + n)
                        turn_memory(n)

                def tile_free(t):
                    pe.wait_ge(hb_ready, 2 * n - 1 + t)

                if first:
                    pe.wait_ge(va_ready, NBLK)
                column_block(m, 0, mt_hi, mt_lo, 2, after, before=before,
                             tile_free=None if first else tile_free, tile0=tile0_done)

            mixer_projection(0, m_wout, True)
            with pe.Fori(1, NBLK) as n:
                mixer_projection(n, m_wout + 2 * n, False)

            def attn_pv(hd):
                pe.wait_ge(vx_l, hd + 1)
                pe.wait_ge(pt_l, hd + 1)
                for d in range(4):
                    for mt in range(2):
                        v_cols = slice(d * P, (d + 1) * P)
                        i = product(tpk[:, d, :], (vx_hi[:, mt, v_cols], vx_lo[:, mt, v_cols]),
                                    (pt_hi[:, mt, :], pt_lo[:, mt, :]), mt == 0, mt == 1)
                i.then_inc(xo_ps, 1)

            def attn_head(hd, m, first):
                def after(c):
                    if c == 1 and not first:
                        attn_pv(hd - 1)
                    if c == 3 and first:
                        pe.wait_ge(mem_lo, NBLK)
                        turn_h(3, 8)
                    if c == 10:
                        pe.wait_ge(kn_ready, hd + 1)
                        if first:
                            pe.wait_ge(blk_lo, 12)
                        else:
                            pe.wait_ge(xo_lo, hd)
                        transpose_block(nat, kx_ps)
                    if c == 17:
                        pe.wait_ge(qn_ready, hd + 1)
                        pe.wait_ge(kx_l, hd + 1)
                        transpose_block(nat, qx_ps)
                    if c == 19:
                        pe.wait_ge(qx_l, hd + 1)
                        for t in range(2):
                            for d in range(4):
                                i = product(tpk[:, t, :], (qx_hi[:, d, tok(t)], qx_lo[:, d, tok(t)]),
                                            (kx_hi[:, d, :], kx_lo[:, d, :]), d == 0, d == 3)
                        i.then_inc(sc_ps, 1)
                    if c == 21:
                        pe.wait_ge(prob_ready, hd + 1)
                        for mt in range(2):
                            for t in range(2):
                                i = pe.transpose(tpk[:, 2 + mt, tok(t)], prob[:, t, tok(mt)],
                                                 ident[:, :])
                        i.then_inc(pt_ps, 1)

                def before(c):
                    if first and c == 6:
                        pe.wait_ge(mem_lo, NBLK)

                if not first:
                    pe.wait_ge(kn_ready, hd)
                column_block(m, 0, yt_hi, yt_lo, 0, after, before=before)
                if first:
                    pe.wait_ge(blk_lo, 12)
                else:
                    pe.wait_ge(qn_ready, hd)
                column_block(m, 8, xt_hi, xt_lo, 2, after)
                if first:
                    pe.wait_ge(sg_ready, NBLK)
                else:
                    pe.wait_ge(vx_l, hd)
                column_block(m, 16, yt_hi, yt_lo, 4, after)

            attn_head(0, m_xattn, True)
            with pe.Fori(1, HEADS) as hd:
                attn_head(hd, m_xattn + 6 * hd, False)

            def attn_projection(n, m, first):
                def before(c):
                    if first and c == 6:
                        pe.wait_ge(xo_lo, HEADS)

                def after(c):
                    if c == 1:
                        if first:
                            attn_pv(HEADS - 1)
                        else:
                            turn_h(n - 1, 12)

                def tile_free(t):
                    pe.wait_ge(hb_ready, 2 * (4 + n) - 1 + t)

                if first:
                    pe.wait_ge(qn_ready, HEADS)
                column_block(m, 0, mt_hi, mt_lo, 2, after, before=before,
                             tile_free=None if first else tile_free, tile0=tile0_done)

            attn_projection(0, m_wo, True)
            with pe.Fori(1, NBLK) as n:
                attn_projection(n, m_wo + 2 * n, False)
            ffn(1)

        @block.gpsimd
        def _(pool):
            def tt(o, a, b, op):
                return pool.tensor_tensor(o, a, b, op)

            def norm_factor(dst, src, ready, count, done):
                pool.wait_ge(ready, count)
                tt(dst[:, :], src[:, :], mhalf[:, :], ALU.pow).then_inc(done, 1)

            for row, v in ((G_MIX, mix_norm), (G_X, xattn_norm),
                           (G_MEM, mem_norm), (G_FFN2, ffn2_norm), (G_D, s5_d)):
                k = v.shape[1] // P
                pool.dma_start(vrow[row:row + k, :],
                               v.rearrange("o (k p) -> (o k) p", p=P)).then_inc(vec_in, 16)
            pool.dma_start(prow[0:32, :], s5_a_re.rearrange("o (j g) p -> (o j) (g p)", g=2)
                           ).then_inc(par_in, 16)
            pool.dma_start(prow[32:64, :], s5_a_im.rearrange("o (j g) p -> (o j) (g p)", g=2)
                           ).then_inc(par_in, 16)
            pool.dma_start(dt_row[64:96, :], s5_log_dt.rearrange("o (j g) -> (o j) g", g=2)
                           ).then_inc(par_in, 16)
            pool.dma_start(parity[:, :], c_parity).then_inc(bc_in, 16)
            for part, (b, c) in enumerate(((s5_b_re, s5_c_re), (s5_b_im, s5_c_im))):
                for g in range(2):
                    pool.dma_start(b_raw[64 * g:64 * g + 64, part, :, :],
                                   b[0].rearrange("(j g) p c -> g p j c", g=2)[g]
                                   ).then_inc(bc_in, 16)
                pool.dma_start(c_raw[:, part, :, :],
                               c[0].rearrange("(q g) c p -> (g c) q p", g=8)).then_inc(bc_in, 16)
            norm_factor(rstd[0], meansq, ms_ready, 1, rstd_ready)

            v = lambda i: par[:, i, :]
            pool.wait_ge(exp_dt, 1)
            tt(v(4), v(0), v(3), ALU.mult)
            tt(v(5), v(1), v(3), ALU.mult)
            pool.drain()
            pool.tensor_scalar(v(6), v(5), 1.0 / (2 * math.pi), ROUND, ALU.mult, ALU.add)
            pool.drain()
            pool.tensor_scalar(v(6), v(6), -ROUND, None, ALU.add)
            pool.drain()
            for k, part in enumerate((TWO_PI_A, TWO_PI_B, TWO_PI_C)):
                pool.tensor_scalar(v(8), v(6), part, None, ALU.mult)
                pool.drain()
                tt(v(7), v(5 if k == 0 else 7), v(8), ALU.subtract)
                pool.drain()
            pool.tensor_scalar(v(7), v(7), math.pi - 1e-6, -(math.pi - 1e-6), ALU.min,
                               ALU.max).then_inc(angles, 1)
            pool.wait_ge(trig, 1)
            tt(v(11), v(9), v(9), ALU.mult)
            pool.drain()
            pool.tensor_scalar(v(12), v(11), -2.0, 1.0, ALU.mult, ALU.add)
            pool.drain()
            tt(v(13), mag[:, :], v(12), ALU.mult)
            tt(v(14), mag[:, :], v(10), ALU.mult)
            tt(v(15), v(0), v(0), ALU.mult)
            tt(v(16), v(1), v(1), ALU.mult)
            pool.drain()
            pool.tensor_scalar(v(13), v(13), -1.0, None, ALU.add)
            tt(v(15), v(15), v(16), ALU.add)
            pool.memset(v(25), -1.0)
            pool.drain()
            tt(v(16), v(15), v(25), ALU.pow)
            for o, a, b in ((17, 13, 0), (18, 14, 1), (19, 14, 0), (20, 13, 1)):
                tt(v(o), v(a), v(b), ALU.mult)
            pool.drain()
            tt(v(21), v(17), v(18), ALU.add)
            tt(v(22), v(19), v(20), ALU.subtract)
            pool.drain()
            tt(v(23), v(21), v(16), ALU.mult)
            tt(v(24), v(22), v(16), ALU.mult)
            pool.drain()

            def complex_product(o_re, o_im, a_re, a_im, b_re, b_im, width):
                t1 = pow_tmp[:, 0, :, 0:width]
                t2 = pow_tmp[:, 1, :, 0:width]
                tt(t1, a_re, b_re, ALU.mult)
                tt(t2, a_im, b_im, ALU.mult)
                pool.drain()
                tt(o_re, t1, t2, ALU.subtract)
                pool.drain()
                tt(t1, a_re, b_im, ALU.mult)
                tt(t2, a_im, b_re, ALU.mult)
                pool.drain()
                tt(o_im, t1, t2, ALU.add)
                pool.drain()

            e_re, e_im = v(12).unsqueeze(2), v(10).unsqueeze(2)
            n_re, n_im = v(5).unsqueeze(2), v(6).unsqueeze(2)
            for re, im in ((2, 3), (0, 1)):
                pool.memset(s5_tab[:, re, :, 0:1], 1.0)
                pool.memset(s5_tab[:, im, :, 0:1], 0.0)
                pool.drain()
                width = 1
                while width < HALF:
                    complex_product(s5_tab[:, re, :, width:2 * width], s5_tab[:, im, :, width:2 * width],
                                    s5_tab[:, re, :, 0:width], s5_tab[:, im, :, 0:width],
                                    e_re.broadcast_to([P, PAIRS, width]),
                                    e_im.broadcast_to([P, PAIRS, width]), width)
                    complex_product(n_re, n_im, e_re, e_im, e_re, e_im, 1)
                    e_re, e_im, n_re, n_im = n_re, n_im, e_re, e_im
                    width *= 2

            pool.wait_ge(bc_in, 16 * 7)
            pool.memset(b_pad[:, :, :, :], 0.0)
            f_re = v(23).unsqueeze(2).broadcast_to([P, PAIRS, HALF])
            f_im = v(24).unsqueeze(2).broadcast_to([P, PAIRS, HALF])
            for part in range(2):
                tt(pow_tmp[:, 0, :, :], f_re, b_raw[:, part, :, :], ALU.mult)
                tt(pow_tmp[:, 1, :, :], f_im, b_raw[:, 1 - part, :, :], ALU.mult)
                pool.drain()
                for g in range(2):
                    half = slice(64 * g, 64 * g + 64)
                    tt(b_pad[half, part, :, HALF * g:HALF * (g + 1)], pow_tmp[half, 0, :, :],
                       pow_tmp[half, 1, :, :], ALU.add if part else ALU.subtract)
                pool.drain()
            for part, sign in ((0, 1.0), (1, -1.0)):
                for g in range(2):
                    i = pool.tensor_scalar(c_pad[:, part, :, 64 * g:64 * g + 64],
                                           c_raw[:, part, :, :], parity[:, g:g + 1], sign,
                                           ALU.mult, ALU.mult)
            i.then_inc(pads_ready, 1)

            norm_factor(rstd[1], meansq, ms_ready, 2, rstd_ready)
            pool.wait_ge(bc_ready, 8)

            def table(pair, buf):
                hi_re = s5_tab[:, 0, ds(pair, 1), :].rearrange("p o (a b) -> p o a b", b=1)
                hi_im = s5_tab[:, 1, ds(pair, 1), :].rearrange("p o (a b) -> p o a b", b=1)
                low = s5_tab[:, 2:4, ds(pair, 1), :].broadcast_to([P, 2, HALF, HALF])
                cs = tab[:, buf, :, :].rearrange("p r (a b) -> p r a b", b=HALF)
                tmp = pool_tmp[:, :, :].rearrange("p r (a b) -> p r a b", b=HALF)
                tt(cs, hi_re.broadcast_to([P, 2, HALF, HALF]), low, ALU.mult)
                tt(tmp, hi_im.broadcast_to([P, 2, HALF, HALF]), low, ALU.mult)
                pool.drain()
                tt(tab[:, buf, 0, :], tab[:, buf, 0, :], pool_tmp[:, 1, :], ALU.subtract)
                tt(tab[:, buf, 1, :], tab[:, buf, 1, :], pool_tmp[:, 0, :],
                   ALU.add).then_inc(tab_ready, 1)
                pool.drain()

            def turn_back(hd, p, first):
                buf = p % 2
                pool.wait_ge(z_ready, 8 * hd + p + 1)
                if not (first and p < 2):
                    pool.wait_ge(y_done, 8 * hd + p - 1)
                z = zb[:, buf, :, :]
                tt(state[:, buf, :, :], z, tab[:, buf, 0:1, :].broadcast_to([P, 2, SEQ]), ALU.mult)
                tt(pool_tmp[:, :, :], z, tab[:, buf, 1:2, :].broadcast_to([P, 2, SEQ]), ALU.mult)
                pool.drain()
                tt(state[:, buf, 0, :], state[:, buf, 0, :], pool_tmp[:, 1, :], ALU.subtract)
                tt(state[:, buf, 1, :], state[:, buf, 1, :], pool_tmp[:, 0, :],
                   ALU.add).then_inc(s_ready, 1)
                pool.drain()

            def head(hd, first, last):
                for p in range(8):
                    if not (last and p == 7):
                        table(8 * hd + p + 1, (p + 1) % 2)
                    turn_back(hd, p, first)
                    if p == 0 and not first:
                        norm_factor(grstd, vare, var_ready, hd, grstd_ready)

            table(0, 0)
            head(0, True, False)
            with pool.Fori(1, HEADS - 1) as hd:
                head(hd, False, False)
            head(HEADS - 1, False, True)
            norm_factor(grstd, vare, var_ready, HEADS, grstd_ready)

            pool.wait_ge(mg_ready, 1)

            def load_mem(n):
                pool.dma_start(memb[:, :, :], mem[0][:, ds(n * COLS, COLS)].rearrange(
                    "(t p) d -> p t d", p=P)).then_inc(mem_in, 16)

            load_mem(0)
            with pool.Fori(1, NBLK) as n:
                pool.wait_ge(mem_ps, n)
                pool.wait_ge(sqm_done, n)
                load_mem(n)
            norm_factor(rstd_mem, meansq_mem, msm_ready, 1, rstdm_ready)
            norm_factor(rstd[2], meansq, ms_ready, 3, rstd_ready)
            norm_factor(rstd[3], meansq, ms_ready, 4, rstd_ready)
            pool.wait_ge(hid_ready[1], 1)
            pool.dma_start(gfin[:, :], final_norm.rearrange("(o d) -> o d", o=1).broadcast_to([P, D])
                           ).then_inc(gfin_in, 16)
            norm_factor(rstd[4], meansq, ms_ready, 5, rstd_ready)


_INS = ['x', 'mem', 'ffn1_norm', 'ffn1_w1', 'ffn1_w3', 'ffn1_w2', 'mix_norm', 'w_in', 's5_a_re',
        's5_a_im', 's5_log_dt', 's5_b_re', 's5_b_im', 's5_c_re', 's5_c_im', 's5_d', 's5_glu_v',
        's5_glu_g', 'ret_w_o', 'w_out', 'xattn_norm', 'mem_norm', 'xattn_wq', 'xattn_wk',
        'xattn_wv', 'xattn_wo', 'ffn2_norm', 'ffn2_w1', 'ffn2_w3', 'ffn2_w2', 'final_norm']
_OUTS = [((1, 256, 2048), 'float32')]


def _constants():
    import numpy as np
    inv = 10000.0 ** (-np.arange(0, 256, 2, dtype=np.float32) / np.float32(256))
    ang = np.arange(256, dtype=np.float32)[:, None] * inv.astype(np.float32)[None, :]
    ang = ang.astype(np.float32).astype(np.float64)
    rope = np.stack([np.cos(ang), np.sin(ang)], 1).reshape(2, 128, 2, 128).transpose(1, 0, 2, 3)
    i = np.arange(256)
    rel = (i[None, :] - i[:, None]).astype(np.float64)
    decay = np.zeros((4, 128, 384))
    for hd in range(4):
        full = np.where(rel >= 0, (1.0 - 2.0 ** (-5.0 - hd)) ** np.maximum(rel, 0), 0.0) / 16.0
        decay[hd, :, 0:256] = full[0:128]
        decay[hd, :, 256:384] = full[128:256, 128:256]
    group = np.arange(128) // 16
    parity = np.stack([group % 2 == 0, group % 2 == 1], 1)
    return {
        "ident": np.eye(128, dtype=np.float32),
        "rope": np.ascontiguousarray(rope, dtype=np.float32),
        "decay": decay.reshape(512, 384).astype(np.float32),
        "parity": parity.astype(np.float32),
    }


def kernel(**inputs):
    import numpy as _np
    import concourse.bacc as _bacc
    from concourse import mybir as _mybir
    from concourse.bass_utils import run_bass_kernel_spmd as _run

    nc = _bacc.Bacc("TRN2", target_bir_lowering=False, num_devices=1)
    arrays, args = {}, []
    for name in _INS:
        a = _np.ascontiguousarray(inputs[name])
        arrays[f"in_{name}_dram"] = a
        args.append(nc.dram_tensor(f"in_{name}_dram", a.shape, _mybir.dt.from_np(a.dtype), kind="ExternalInput").ap())
    for name, a in _constants().items():
        arrays[f"c_{name}_dram"] = a
        args.append(nc.dram_tensor(f"c_{name}_dram", a.shape, _mybir.dt.from_np(a.dtype), kind="ExternalInput").ap())
    for i, (shape, dtype) in enumerate(_OUTS):
        dt = _mybir.dt.from_np(_np.dtype(dtype))
        args.append(nc.dram_tensor(f"out_{i}_dram", shape, dt, kind="ExternalOutput").ap())
    build(nc, *args)
    r = _run(nc, [arrays], core_ids=[0])
    return r.results[0]["out_0_dram"]
```
